# Optimizing a Trainium2 kernel written in Bass

```python
import math
import jax, jax.numpy as jnp
from jax import lax
import numpy as np

D_MODEL = 1024
BATCH = 1
SEQ = 256
DEPTH = 2

CHUNK = 64
N_META = 16
BLOCK = 128
N_MIXERS = 3
HEAD_DIM = 64
N_HEADS = D_MODEL // HEAD_DIM
N_KV_HEADS = 4
KV_GROUP = N_HEADS // N_KV_HEADS
KV_DIM = N_KV_HEADS * HEAD_DIM
WINDOW = 128
WINDOW_CHUNKS = WINDOW // CHUNK
ROPE_THETA = 10000.0
D_LRU = D_MODEL
LRU_BLOCK = 256
N_LRU_BLOCKS = D_LRU // LRU_BLOCK
CONV_WIDTH = 4
LRU_C = 8.0
D_FF = 2816
RMS_EPS = 1e-6
N_SB = len(range(0, DEPTH, N_MIXERS))
N_SWA = len(range(1, DEPTH, N_MIXERS))
N_LRU = len(range(2, DEPTH, N_MIXERS))

kernel_name = "hybrid_chunk_causal_sb_swa_rglru_macaron"

def rms_norm(x, g):
    xf = x.astype(jnp.float32)
    y = xf * lax.rsqrt(jnp.mean(xf * xf, axis=-1, keepdims=True) + RMS_EPS)
    return (y * g.astype(jnp.float32)).astype(x.dtype)

def swiglu(x, w_gate, w_up, w_down):
    return (jax.nn.silu(x @ w_gate) * (x @ w_up)) @ w_down

def rope(t, pos):
    half = HEAD_DIM // 2
    inv_freq = ROPE_THETA ** (-jnp.arange(half, dtype=jnp.float32) / half)
    ang = pos[:, None] * inv_freq[None, :]
    cos = jnp.cos(ang)[None, :, None, :]
    sin = jnp.sin(ang)[None, :, None, :]
    tf = t.astype(jnp.float32)
    t1, t2 = tf[..., :half], tf[..., half:]
    return jnp.concatenate([t1 * cos - t2 * sin, t2 * cos + t1 * sin], axis=-1).astype(t.dtype)

def stick_breaking_mixer(h, w_in, w_out):
    B, L, _ = h.shape
    nb = -(-L // BLOCK)
    Lp = nb * BLOCK
    pad = ((0, 0), (0, Lp - L), (0, 0))
    q, k, v = [jnp.pad(t, pad).reshape(B, Lp, N_HEADS, HEAD_DIM)
               for t in jnp.split(h @ w_in, 3, axis=-1)]
    q_blocks = q.reshape(B, nb, BLOCK, N_HEADS, HEAD_DIM).transpose(1, 0, 2, 3, 4)
    k_pos = jnp.arange(Lp)
    scale = HEAD_DIM ** -0.5

    def one_block(args):
        b, qb = args
        q_pos = b * BLOCK + jnp.arange(BLOCK)
        z = jnp.einsum('bqhd,bkhd->bhqk', qb, k,
                       preferred_element_type=jnp.float32) * scale
        visible = k_pos[None, :] < q_pos[:, None]
        log_stay = jnp.where(visible, jax.nn.log_sigmoid(-z), 0.0)
        log_pass = lax.cumsum(log_stay, axis=3, reverse=True) - log_stay
        w = jnp.where(visible, jnp.exp(jax.nn.log_sigmoid(z) + log_pass), 0.0)
        return jnp.einsum('bhqk,bkhd->bqhd', w.astype(v.dtype), v)

    o = lax.map(one_block, (jnp.arange(nb), q_blocks))
    o = o.transpose(1, 0, 2, 3, 4).reshape(B, Lp, D_MODEL)[:, :L]
    return o @ w_out

def swa_sink_mixer(h, w_in, sinks, w_out, pos):
    B, L, _ = h.shape
    n_chunks = (L - N_META) // CHUNK
    q, k, v = jnp.split(h @ w_in, [D_MODEL, D_MODEL + KV_DIM], axis=-1)
    q = rope(q.reshape(B, L, N_HEADS, HEAD_DIM), pos).reshape(B, L, N_KV_HEADS, KV_GROUP, HEAD_DIM)
    k = rope(k.reshape(B, L, N_KV_HEADS, HEAD_DIM), pos)
    v = v.reshape(B, L, N_KV_HEADS, HEAD_DIM)
    scale = HEAD_DIM ** -0.5
    k_meta, v_meta = k[:, :N_META], v[:, :N_META]
    sink_logit = sinks.astype(jnp.float32).reshape(N_KV_HEADS, KV_GROUP, 1, 1)

    qf = q[:, N_META:].reshape(B, n_chunks, CHUNK, N_KV_HEADS, KV_GROUP, HEAD_DIM)

    def band(t):
        tc = t[:, N_META:].reshape(B, n_chunks, CHUNK, N_KV_HEADS, HEAD_DIM)
        tp = jnp.pad(tc, ((0, 0), (WINDOW_CHUNKS - 1, 0), (0, 0), (0, 0), (0, 0)))
        return jnp.concatenate([tp[:, j:j + n_chunks] for j in range(WINDOW_CHUNKS)], axis=2)

    k_band, v_band = band(k), band(v)
    key_chunk = (jnp.arange(n_chunks)[:, None] - (WINDOW_CHUNKS - 1)
                 + jnp.repeat(jnp.arange(WINDOW_CHUNKS), CHUNK)[None, :])
    visible = (key_chunk >= 0)[None, :, None, None, None, :]
    s_meta = jnp.einsum('bnqhgd,bmhd->bnhgqm', qf, k_meta,
                        preferred_element_type=jnp.float32) * scale
    s_band = jnp.einsum('bnqhgd,bnkhd->bnhgqk', qf, k_band,
                        preferred_element_type=jnp.float32) * scale
    s_band = jnp.where(visible, s_band, -jnp.inf)
    sink = jnp.broadcast_to(sink_logit, s_meta.shape[:-1] + (1,))
    p = jax.nn.softmax(jnp.concatenate([s_meta, s_band, sink], axis=-1), axis=-1)
    p_meta = p[..., :N_META].astype(v.dtype)
    p_band = p[..., N_META:N_META + WINDOW_CHUNKS * CHUNK].astype(v.dtype)
    o_frames = (jnp.einsum('bnhgqm,bmhd->bnqhgd', p_meta, v_meta)
                + jnp.einsum('bnhgqk,bnkhd->bnqhgd', p_band, v_band))

    qm = q[:, :N_META]
    s_mm = jnp.einsum('bqhgd,bmhd->bhgqm', qm, k_meta,
                      preferred_element_type=jnp.float32) * scale
    sink_m = jnp.broadcast_to(sink_logit, s_mm.shape[:-1] + (1,))
    p_m = jax.nn.softmax(jnp.concatenate([s_mm, sink_m], axis=-1), axis=-1)
    o_meta = jnp.einsum('bhgqm,bmhd->bqhgd', p_m[..., :N_META].astype(v.dtype), v_meta)

    o = jnp.concatenate([o_meta.reshape(B, N_META, D_MODEL),
                         o_frames.reshape(B, L - N_META, D_MODEL)], axis=1)
    return o @ w_out

def rglru_mixer(h, w_in, conv_w, conv_b, w_a, b_a, w_x, b_x, lam, w_out):
    B, L, _ = h.shape
    gate, xr = jnp.split(h @ w_in, 2, axis=-1)
    xp = jnp.pad(xr, ((0, 0), (CONV_WIDTH - 1, 0), (0, 0)))
    xc = conv_b + sum(xp[:, j:j + L] * conv_w[j] for j in range(CONV_WIDTH))
    xb = xc.reshape(B, L, N_LRU_BLOCKS, LRU_BLOCK)
    r = jax.nn.sigmoid(jnp.einsum('blni,nij->blnj', xb, w_a).reshape(B, L, D_LRU) + b_a)
    i_gate = jax.nn.sigmoid(jnp.einsum('blni,nij->blnj', xb, w_x).reshape(B, L, D_LRU) + b_x)
    log_a = (-LRU_C * jax.nn.softplus(-lam) * r).astype(jnp.float32)
    a = jnp.exp(log_a)
    u = jnp.sqrt(-jnp.expm1(2.0 * log_a)) * (i_gate * xc).astype(jnp.float32)

    def combine(left, right):
        a_l, b_l = left
        a_r, b_r = right
        return a_l * a_r, a_r * b_l + b_r

    _, hs = lax.associative_scan(combine, (a, u), axis=1)
    y = hs.astype(h.dtype) * jax.nn.gelu(gate)
    return y @ w_out

def setup_inputs(seed: int = 0) -> dict:
    key = jax.random.key(seed)
    ks = jax.random.split(key, 20)

    def nrm(k, shape, fan_in):
        return jax.random.normal(k, shape, jnp.float32) * fan_in ** -0.5

    u = jax.random.uniform(ks[18], (N_LRU, D_LRU), jnp.float32, minval=0.9, maxval=0.999)
    a_base = u ** (1.0 / LRU_C)
    lru_lambda = jnp.log(a_base) - jnp.log1p(-a_base)
    return {
        "x": jax.random.normal(ks[0], (BATCH, SEQ, D_MODEL), jnp.float32),
        "meta_tokens": jax.random.normal(ks[1], (N_META, D_MODEL), jnp.float32),
        "norm_g": 1.0 + 0.05 * jax.random.normal(ks[2], (DEPTH, 6, D_MODEL), jnp.float32),
        "ffn_w_gate": nrm(ks[3], (DEPTH, 2, D_MODEL, D_FF), D_MODEL),
        "ffn_w_up": nrm(ks[4], (DEPTH, 2, D_MODEL, D_FF), D_MODEL),
        "ffn_w_down": nrm(ks[5], (DEPTH, 2, D_FF, D_MODEL), D_FF),
        "sb_w_in": nrm(ks[6], (N_SB, D_MODEL, 3 * D_MODEL), D_MODEL),
        "sb_w_out": nrm(ks[7], (N_SB, D_MODEL, D_MODEL), D_MODEL),
        "swa_w_in": nrm(ks[8], (N_SWA, D_MODEL, D_MODEL + 2 * KV_DIM), D_MODEL),
        "swa_sinks": 0.5 * jax.random.normal(ks[9], (N_SWA, N_HEADS), jnp.float32),
        "swa_w_out": nrm(ks[10], (N_SWA, D_MODEL, D_MODEL), D_MODEL),
        "lru_w_in": nrm(ks[11], (N_LRU, D_MODEL, 2 * D_LRU), D_MODEL),
        "lru_conv_w": nrm(ks[12], (N_LRU, CONV_WIDTH, D_LRU), CONV_WIDTH),
        "lru_conv_b": 0.01 * jax.random.normal(ks[13], (N_LRU, D_LRU), jnp.float32),
        "lru_w_a": nrm(ks[14], (N_LRU, N_LRU_BLOCKS, LRU_BLOCK, LRU_BLOCK), LRU_BLOCK),
        "lru_b_a": 0.01 * jax.random.normal(ks[15], (N_LRU, D_LRU), jnp.float32),
        "lru_w_x": nrm(ks[16], (N_LRU, N_LRU_BLOCKS, LRU_BLOCK, LRU_BLOCK), LRU_BLOCK),
        "lru_b_x": 0.01 * jax.random.normal(ks[17], (N_LRU, D_LRU), jnp.float32),
        "lru_lambda": lru_lambda,
        "lru_w_out": nrm(ks[19], (N_LRU, D_LRU, D_MODEL), D_LRU),
    }

def reference(x, meta_tokens, norm_g, ffn_w_gate, ffn_w_up, ffn_w_down,
              sb_w_in, sb_w_out, swa_w_in, swa_sinks, swa_w_out,
              lru_w_in, lru_conv_w, lru_conv_b, lru_w_a, lru_b_a, lru_w_x, lru_b_x,
              lru_lambda, lru_w_out):
    B = x.shape[0]
    meta = jnp.broadcast_to(meta_tokens[None].astype(x.dtype), (B, N_META, D_MODEL))
    h = jnp.concatenate([meta, x], axis=1)
    L = h.shape[1]
    pos = jnp.arange(L, dtype=jnp.float32)
    for i in range(DEPTH):
        g = norm_g[i]
        f = swiglu(rms_norm(h, g[0]), ffn_w_gate[i, 0], ffn_w_up[i, 0], ffn_w_down[i, 0])
        h = h + 0.5 * rms_norm(f, g[1])
        m = rms_norm(h, g[2])
        kind, j = i % N_MIXERS, i // N_MIXERS
        if kind == 0:
            m = stick_breaking_mixer(m, sb_w_in[j], sb_w_out[j])
        elif kind == 1:
            m = swa_sink_mixer(m, swa_w_in[j], swa_sinks[j], swa_w_out[j], pos)
        else:
            m = rglru_mixer(m, lru_w_in[j], lru_conv_w[j], lru_conv_b[j], lru_w_a[j],
                            lru_b_a[j], lru_w_x[j], lru_b_x[j], lru_lambda[j], lru_w_out[j])
        h = h + rms_norm(m, g[3])
        f = swiglu(rms_norm(h, g[4]), ffn_w_gate[i, 1], ffn_w_up[i, 1], ffn_w_down[i, 1])
        h = h + 0.5 * rms_norm(f, g[5])
    return h[:, N_META:]


_drawn_inputs = setup_inputs


def setup_inputs(seed=0):
    import zlib

    import numpy as np

    out = dict(_drawn_inputs(seed))
    spreads = {}
    factors = {'swa_sinks': 8.0}
    for name, (base, spread) in spreads.items():
        noise = np.random.default_rng([zlib.crc32(name.encode()), seed]).standard_normal(out[name].shape)
        drawn = base * np.exp(spread * noise) if base else spread * noise
        out[name] = __import__('jax').numpy.asarray(drawn.astype(out[name].dtype))
    for name, factor in factors.items():
        out[name] = (out[name] * factor).astype(out[name].dtype)
    return out
```

```python
from contextlib import ExitStack

import numpy as np

import concourse.bass as bass
from concourse import mybir

P = 128
D = 1024
KT = D // P
SEQ = 256
META = 16
L = META + SEQ
DEPTH = 2
FF = 2816
HD = 64
NH = D // HD
NKV = 4
GROUP = NH // NKV
CHUNK = 64
THETA = 10000.0
EPS = 1e-6
SCALE = HD ** -0.5
HIDDEN = -1e30

PW = 2048
RAW_SLOTS = 2
SLOTS = 4
HALF = PW // 2

SB_KEY = [0, 128, L - P]
SB_Q0 = [0, 128, 256]
SB_COL = [0, 272, 416]
SB_W = 432
SW_KEYS = [144, 272]
SW_COL = [0, 144]
SW_W = 416

CONST = {}
_at = 0
for _n, _w in (("ident", P), ("ones", P), ("mask_sb", SB_W), ("tri", P), ("mask_sw", SW_W),
               ("rot", P), ("cos", L), ("sin", L)):
    CONST[_n] = (_at, _at + _w)
    _at += _w
CONST_W = _at
FEW = 2 * P

F32 = mybir.dt.float32
F32R = mybir.dt.float32r
ALU = mybir.AluOpType
ACT = mybir.ActivationFunctionType
AX = mybir.AxisListType


class Sub:

    def __init__(self, u, kind, g0, n_in, n_out, t_in, t_out):
        self.u, self.kind, self.g0, self.n_in, self.n_out = u, kind, g0, n_in, n_out
        self.layer, self.part = u // 3, u % 3
        self.pre = (self.layer * 6 + 2 * self.part) * KT
        self.post = self.pre + KT
        self.t_in, self.t_out = t_in, t_out
        self.factor = 1.0 if self.part == 1 else 0.5
        self.g_out = g0 + n_in
        self.end = g0 + n_in + n_out


def plan():
    subs, g = [], 0
    for u, (kind, n_in, n_out) in enumerate([("ffn", 22, 11), ("sb", 12, 4), ("ffn", 22, 11),
                                             ("ffn", 22, 11), ("swa", 6, 4), ("ffn", 22, 11)]):
        subs.append(Sub(u, kind, g, n_in, n_out, META if u == 5 else 0, META if u >= 4 else 0))
        g += n_in + n_out
    return subs, g


SUBS, PANELS = plan()
BANK_IN = [(0, 1), (2, 3), (4, 5), (6, 7)]
BANK_OUT = [4, 5, 6, 7, 0, 1, 2, 3]
BANK_POST, BANK_PRE = 6, 7
HEAD = 3


def build(nc, x_in, meta_in, norm_g, w_gate, w_up, w_down, sb_w_in, sb_w_out,
          swa_w_in, swa_sinks, swa_w_out, const_in, out):
    ctx = ExitStack()
    with ctx:
        def sb(name, shape, dt=F32):
            return ctx.enter_context(nc.sbuf_tensor(name, shape, dt))

        def sem(name):
            return ctx.enter_context(nc.semaphore(name))

        ps = ctx.enter_context(nc.psum_tensor("ps", [P, 8, 512], F32))
        const = sb("const", [P, CONST_W])
        raw = sb("raw", [P, RAW_SLOTS, PW])
        w_hi = sb("w_hi", [P, SLOTS, PW], F32R)
        w_lo = sb("w_lo", [P, SLOTS, PW], F32R)
        xT = sb("xT", [P, KT, L])
        y_hi = sb("y_hi", [P, KT, L], F32R)
        y_lo = sb("y_lo", [P, KT, L], F32R)
        fT = sb("fT", [P, KT, L])
        sq = sb("sq", [P, KT, L])
        gains = sb("gains", [P, DEPTH * 6 * KT])
        sinks = sb("sinks", [P, NH])
        rms_inv = sb("rms_inv", [P, L])
        pre_ms = sb("pre_ms", [P, L])
        pre_ln = sb("pre_ln", [P, L])
        eps_ms = sb("eps_ms", [P, L])
        post_ms = sb("post_ms", [P, L])
        post_ln = sb("post_ln", [P, L])
        post_f = sb("post_f", [P, L])
        scaled = sb("scaled", [P, 2, L])
        g_rows = sb("g_rows", [DEPTH * 6 * KT, P])
        s_row = sb("s_row", [1, NH])

        with ExitStack() as over:
            def ffn_sb(name, shape, dt=F32):
                return over.enter_context(nc.sbuf_tensor(name, shape, dt))
            h_hi = ffn_sb("h_hi", [P, FF // P, L], F32R)
            h_lo = ffn_sb("h_lo", [P, FF // P, L], F32R)
            act = ffn_sb("act", [P, 2, 2, L])
            hid = ffn_sb("hid", [P, 2, 2, L])
        with ExitStack() as over:
            def mix_sb(name, shape, dt=F32):
                return over.enter_context(nc.sbuf_tensor(name, shape, dt))
            qkv = mix_sb("qkv", [P, 3 * KT, L])
            v_tok = mix_sb("v_tok", [P, 3, D])
            z = mix_sb("z", [P, 4, SB_W])
            e = mix_sb("e", [P, 2, SB_W])
            sp = mix_sb("sp", [P, 2, SB_W])
            w = mix_sb("w", [P, 3, SB_W])
        with ExitStack() as over:
            def swa_sb(name, shape, dt=F32):
                return over.enter_context(nc.sbuf_tensor(name, shape, dt))
            swa_sb("under_qkv", [P, 12, L])
            kd = swa_sb("kd", [P, NKV, L])
            vt = swa_sb("vt", [P, 3, NKV * HD])
            rot_s = swa_sb("rot_s", [P, 2, 2, L])
            rot_c = swa_sb("rot_c", [P, 2, 2, L])
            s = swa_sb("s", [P, 2, GROUP, SW_W])
            p_t = swa_sb("p_t", [P, 2, 384])
            p_t16 = swa_sb("p_t16", [META, 2, 256])
            top = swa_sb("top", [P, 2, 2, GROUP])
            neg = swa_sb("neg", [P, 2, 2, GROUP])
            tot = swa_sb("tot", [P, 2, 2, GROUP])
            snk = swa_sb("snk", [P, 2, 2, GROUP])
            den = swa_sb("den", [P, 2, 2, GROUP])
            inv = swa_sb("inv", [P, 2, 2, GROUP])

        def cst(name, rows=P, a=0, b=None):
            lo, hi = CONST[name]
            return const[0:rows, lo + a:(hi if b is None else lo + b)]

        def spread(ap, n, t0):
            return ap[:, t0:L].unsqueeze(1).broadcast_to([P, n, L - t0])

        def x_rows(t):
            return t[:].rearrange("p a b -> p (a b)")[:, 0:2 * D].rearrange("p (a n) -> p a n", a=2)

        def meta_rows(t):
            return t[0:META].rearrange("p a b -> p (a b)")[:, 0:D]

        few_landed = sem("few_landed")
        const_in_sem = sem("const_landed")
        x_landed = sem("x_landed")
        small_landed = sem("small_landed")
        raw_landed = [sem(f"raw_landed{i}") for i in range(RAW_SLOTS)]
        hi_ready = sem("hi_ready")
        lo_ready = sem("lo_ready")
        panel_done = sem("panel_done")
        small_T = sem("small_T")
        small_ready = sem("small_ready")
        x_turned = sem("x_turned")
        gate_ready = sem("gate_ready")
        silu_ready = sem("silu_ready")
        h_ready = sem("h_ready")
        hh_ready = sem("hh_ready")
        hl_ready = sem("hl_ready")
        f_done = sem("f_done")
        f_sq = sem("f_sq")
        f_saved = sem("f_saved")
        f_saved2 = sem("f_saved2")
        f_acc = sem("f_acc")
        post_sum = sem("post_sum")
        post_var = sem("post_var")
        post_log = sem("post_log")
        eps_ready = sem("eps_ready")
        post_ready = sem("post_ready")
        u_ready = sem("u_ready")
        x_ready = sem("x_ready")
        yh_ready = sem("yh_ready")
        yl_ready = sem("yl_ready")
        x_sq = sem("x_sq")
        x_acc = sem("x_acc")
        pre_sum = sem("pre_sum")
        pre_var = sem("pre_var")
        pre_log = sem("pre_log")
        rms_ready = sem("rms_ready")
        proj_drained = sem("proj_drained")
        v_turned = sem("v_turned")
        v_saved_a = sem("v_saved_a")
        v_saved_d = sem("v_saved_d")
        z_done = sem("z_done")
        z_ready = sem("z_ready")
        e_abs = sem("e_abs")
        e_exp = sem("e_exp")
        e_ln = sem("e_ln")
        sp_ready = sem("sp_ready")
        c_done = sem("c_done")
        d_ready = sem("d_ready")
        w_ready = sem("w_ready")
        o_done = sem("o_done")
        oh_ready = sem("oh_ready")
        ol_ready = sem("ol_ready")
        rot_done = sem("rot_done")
        rs_ready = sem("rs_ready")
        rc_ready = sem("rc_ready")
        roped = sem("roped")
        s_done = sem("s_done")
        s_ready = sem("s_ready")
        top_ready = sem("top_ready")
        p_exp = sem("p_exp")
        stat = sem("stat")
        snk_sum = sem("snk_sum")
        snk_exp = sem("snk_exp")
        p_ready = sem("p_ready")
        pt_done = sem("pt_done")
        pt_saved = sem("pt_saved")
        pt16_saved = sem("pt16_saved")
        out_turned = sem("out_turned")
        out_a = sem("out_a")
        out_d = sem("out_d")
        out_stored = sem("out_stored")

        pairs_before = [11 * sum(1 for t in SUBS[:u] if t.kind == "ffn") for u in range(7)]
        drained_before = [sum(t.n_in for t in SUBS[:u] if t.kind != "ffn") for u in range(7)]

        def steps(eng, n, body):
            if n >= 8:
                with eng.Fori(0, n // 4) as it:
                    for i in range(4):
                        body(i, it)
                rest = range(n // 4 * 4, n)
            else:
                rest = range(n)
            for i in rest:
                body(i, 0)

        def n_split(t):
            return min(t.n_out - 1, PANELS - t.g_out - SLOTS)

        block = ctx.enter_context(nc.Block())

        @block.sync
        def _(sp_eng):
            sp_eng.dma_start(x_rows(sq), x_in.rearrange("(a p) d -> p a d", p=P)).then_inc(x_landed, 16)

            def load(g, more, src):
                if g >= RAW_SLOTS:
                    sp_eng.wait_ge(lo_ready, 2 * (g - RAW_SLOTS + 1) + 2 * more)
                sp_eng.dma_start(raw[:, g % RAW_SLOTS, :].rearrange("p (k n) -> p k n", n=src.shape[-1]), src)\
                      .then_inc(raw_landed[g % RAW_SLOTS], 16)

            def columns(wt, i):
                return wt.rearrange("(k p) n -> p k n", p=P)[:, :, bass.ds(256 * i, 256)]

            def rows(wt, i):
                return wt.rearrange("(r c p) n -> p r c n", c=2, p=P)[:, bass.ds(i, 1)].rearrange(
                    "p r c n -> p (r c) n")

            def pairs(lo, n, body):
                with sp_eng.Fori(0, n // 2) as it:
                    for c in range(2):
                        body(lo + c, 2 * it, 2 * it + c)
                if n % 2:
                    body(lo + n - 1, 0, n - 1)

            for t in SUBS:
                if t.kind == "ffn":
                    j = t.part // 2
                    if t.u == 0:
                        load(0, 0, columns(w_gate[0, 0], 0))
                        load(1, 0, columns(w_up[0, 0], 0))
                        with sp_eng.Fori(1, 11) as it:
                            load(2, 2 * it - 2, columns(w_gate[0, 0], it))
                            load(3, 2 * it - 2, columns(w_up[0, 0], it))
                    else:
                        with sp_eng.Fori(0, 11) as it:
                            load(t.g0, 2 * it, columns(w_gate[t.layer, j], it))
                            load(t.g0 + 1, 2 * it, columns(w_up[t.layer, j], it))
                    pairs(t.g_out, 11, lambda g, more, i: load(g, more, rows(w_down[t.layer, j], i)))
                else:
                    w_in, w_out = (sb_w_in[0], sb_w_out[0]) if t.kind == "sb" else (swa_w_in[0], swa_w_out[0])
                    pairs(t.g0, t.n_in, lambda g, more, i: load(g, more, columns(w_in, i)))
                    pairs(t.g_out, t.n_out, lambda g, more, i: load(g, more, rows(w_out, i)))

            out_v = out.rearrange("(a p) d -> a p d", p=P)
            for n in range(4):
                a, half = n // 2, n % 2
                if n % 2 == 0:
                    sp_eng.wait_ge(out_a, n // 2 + 1)
                else:
                    sp_eng.wait_ge(out_d, n // 2 + 1)
                sp_eng.dma_start(out_v[a, :, 512 * half:512 * half + 512],
                                 x_rows(sq)[:, a, 512 * half:512 * half + 512]).then_inc(out_stored, 16)
            sp_eng.wait_ge(out_stored, 64)

        @block.gpsimd
        def _(pool):
            pool.wait_ge(const_in_sem, 16)
            for b in range(5):
                pool.wait_ge(proj_drained, drained_before[4] + b + 1)
                if b >= 2:
                    pool.wait_ge(roped, b - 1)
                nc.gpsimd.tensor_tensor(rot_c[:, b % 2], qkv[:, 2 * b:2 * b + 2, :],
                                        spread(cst("cos"), 2, 0), ALU.mult).then_inc(rc_ready, 1)

        @block.scalar
        def _(a):
            def conv_hi(g, it=0):
                if g >= PANELS:
                    return
                a.wait_ge(raw_landed[g % RAW_SLOTS], 16 * (g // RAW_SLOTS + 1) + 32 * it)
                if g >= SLOTS:
                    a.wait_ge(panel_done, g - SLOTS + 1 + 4 * it)
                for c in range(2):
                    part = slice(c * HALF, (c + 1) * HALF)
                    nc.scalar.copy(w_hi[:, g % SLOTS, part], raw[:, g % RAW_SLOTS, part]).then_inc(hi_ready, 1)

            def split_y(b):
                t0 = SUBS[b].t_in
                for d in range(KT):
                    a.wait_ge(x_ready, KT * b + d + 1)
                    nc.scalar.activation(y_hi[:, d, t0:L], xT[:, d, t0:L], ACT.Copy,
                                         scale=gains[:, SUBS[b].pre + d:SUBS[b].pre + d + 1]).then_inc(yh_ready, 1)
                    if b == 0 and d == 3:
                        conv_hi(0)
                if b == 0:
                    conv_hi(1)
                    conv_hi(2)
                for c in range(2):
                    nc.scalar.activation(fT[:, 4 * c:4 * c + 4, t0:L], xT[:, 4 * c:4 * c + 4, t0:L],
                                         ACT.Square).then_inc(x_sq, 1)
                conv_hi(SUBS[b].g0 + 3)
                a.wait_ge(pre_var, b + 1)
                nc.scalar.activation(pre_ln[:, t0:L], pre_ms[:, t0:L], ACT.Ln).then_inc(pre_log, 1)
                a.wait_ge(pre_log, b + 1)
                nc.scalar.activation(rms_inv[:, t0:L], pre_ln[:, t0:L], ACT.Exp, scale=-0.5).then_inc(rms_ready, 1)
                if SUBS[b].kind == "ffn":
                    nc.scalar.preload_act_table_set("silu_and_others")

            a.dma_start(const[:, 0:FEW], const_in[:, 0:FEW]).then_inc(few_landed, 16)
            a.dma_start(g_rows[:], norm_g.rearrange("l n (k p) -> (l n k) p", p=P)).then_inc(small_landed, 16)
            a.dma_start(s_row[:], swa_sinks).then_inc(small_landed, 16)
            a.dma_start(meta_rows(fT), meta_in).then_inc(x_landed, 16)
            a.dma_start(const[:, FEW:CONST_W], const_in[:, FEW:CONST_W]).then_inc(const_in_sem, 16)
            nc.scalar.preload_act_table_set("natural_log_exp_and_others")
            a.wait_ge(small_T, 1)
            nc.scalar.copy(gains[:], ps[:, 0, 288:288 + 96]).then_inc(small_ready, 1)
            nc.scalar.copy(sinks[:], ps[:, 1, 288:288 + NH]).then_inc(small_ready, 1)
            a.wait_ge(small_ready, 2)
            split_y(0)

            for t in SUBS:
                if t.kind == "ffn":
                    base = pairs_before[t.u]

                    def in_step(i, it):
                        conv_hi(t.g0 + i + 4, it)
                        j = i // 2
                        if i % 2 == 0:
                            a.wait_ge(gate_ready, base + j + 1 + 2 * it)
                            nc.scalar.activation(act[:, j % 2, :, t.t_in:L], act[:, j % 2, :, t.t_in:L],
                                                 ACT.Silu).then_inc(silu_ready, 1)
                        else:
                            a.wait_ge(h_ready, base + j + 1 + 2 * it)
                            nc.scalar.copy(h_hi[:, bass.ds(2 * j + 4 * it, 2), t.t_in:L],
                                           hid[:, j % 2, :, t.t_in:L]).then_inc(hh_ready, 1)
                    steps(a, 22, in_step)
                elif t.kind == "sb":
                    steps(a, t.n_in, lambda i, it: conv_hi(t.g0 + i + 4, it))
                    for n in range(0, 6, 2):
                        a.wait_ge(v_turned, n + 1)
                        nc.scalar.copy(v_tok[:, n // 2, 0:512], ps[:, 2 + n, :]).then_inc(v_saved_a, 1)
                    for st in range(NH + 5):
                        if st < NH:
                            a.wait_ge(e_abs, st + 1)
                            nc.scalar.activation(e[:, st % 2], e[:, st % 2], ACT.Exp).then_inc(e_exp, 1)
                        if 3 <= st < NH + 3:
                            h = st - 3
                            a.wait_ge(d_ready, h + 1)
                            nc.scalar.activation(w[:, h % 3], w[:, h % 3], ACT.Exp).then_inc(w_ready, 1)
                        if st < NH:
                            a.wait_ge(e_exp, st + 1)
                            nc.scalar.activation(e[:, st % 2], e[:, st % 2], ACT.Ln, bias=1.0).then_inc(e_ln, 1)
                        if st >= 5 and (st - 5) % 2 == 1:
                            q = (st - 5) // 2
                            a.wait_ge(o_done, 2 * q + 2)
                            nc.scalar.copy(y_hi[:, q, :], ps[:, 4 + q % 2, 0:L]).then_inc(oh_ready, 1)
                else:
                    steps(a, t.n_in, lambda i, it: conv_hi(t.g0 + i + 4, it))
                    a.wait_ge(v_turned, 7)
                    nc.scalar.copy(vt[:, 0:2, :], ps[:, 6, :].rearrange("p (a b) -> p a b", a=2)).then_inc(v_saved_a, 1)

                    def exps(gq):
                        a.wait_ge(top_ready, gq + 1)
                        for h in range(GROUP):
                            for c in range(2):
                                k0, k1 = SW_COL[c], SW_COL[c] + SW_KEYS[c]
                                nc.scalar.activation(s[:, gq % 2, h, k0:k1], s[:, gq % 2, h, k0:k1], ACT.Exp,
                                                     bias=neg[:, gq % 2, c, h:h + 1],
                                                     accum_out=tot[:, gq % 2, c, h:h + 1]).then_inc(p_exp, 1)
                        a.wait_ge(snk_sum, gq + 1)
                        nc.scalar.activation(snk[:, gq % 2], snk[:, gq % 2], ACT.Exp).then_inc(snk_exp, 1)

                    def save_pt(h):
                        a.wait_ge(pt_done, h + 1)
                        if h >= 2:
                            a.wait_ge(o_done, NH + h - 1)
                        nc.scalar.copy(p_t[:, h % 2], ps[:, 4 + h % 2, 0:384]).then_inc(pt_saved, 1)

                    def save_o(q):
                        a.wait_ge(o_done, NH + 2 * q + 2)
                        nc.scalar.copy(y_hi[:, q, META:L], ps[:, 2 + q % 2, 0:256])\
                            .then_inc(oh_ready, 1)
                    exps(0)
                    for gq in range(NKV):
                        if gq + 1 < NKV:
                            exps(gq + 1)
                        for h in range(GROUP * gq, GROUP * gq + GROUP):
                            save_pt(h)
                            if h % 2 == 0 and h >= 2:
                                save_o(h // 2 - 1)
                    save_o(NH // 2 - 1)

                if t.kind == "ffn":
                    nc.scalar.preload_act_table_set("natural_log_exp_and_others")
                steps(a, n_split(t), lambda i, it: conv_hi(t.g_out + i + 4, it))
                k = t.u
                t0 = t.t_out
                for n in range(3):
                    a.wait_ge(f_done, KT * k + 2 * n + 2)
                    b0 = BANK_OUT[2 * n]
                    nc.scalar.activation(sq[:, 2 * n:2 * n + 2, t0:L], ps[:, b0:b0 + 2, t0:L], ACT.Square)\
                        .then_inc(f_sq, 1)
                    nc.scalar.copy(fT[:, 2 * n:2 * n + 2, t0:L], ps[:, b0:b0 + 2, t0:L]).then_inc(f_saved, 1)
                for d in range(6, 8):
                    a.wait_ge(f_done, KT * k + d + 1)
                    nc.scalar.activation(sq[:, d, t0:L], ps[:, BANK_OUT[d], t0:L], ACT.Square).then_inc(f_sq, 1)
                a.wait_ge(post_var, k + 1)
                nc.scalar.activation(post_ln[:, t0:L], post_ms[:, t0:L], ACT.Ln,
                                     scale=t.factor ** -2).then_inc(post_log, 1)
                a.wait_ge(post_log, k + 1)
                nc.scalar.activation(post_f[:, t0:L], post_ln[:, t0:L], ACT.Exp, scale=-0.5).then_inc(post_ready, 1)
                if t.u < 5:
                    split_y(t.u + 1)
                else:
                    for n in range(0, 4, 2):
                        a.wait_ge(out_turned, n + 1)
                        nc.scalar.copy(x_rows(sq)[:, n // 2, 0:512], ps[:, n, :]).then_inc(out_a, 1)

        @block.vector
        def _(v):
            def conv_lo(g, it=0):
                if g >= PANELS:
                    return
                for c in range(2):
                    part = slice(c * HALF, (c + 1) * HALF)
                    v.wait_ge(hi_ready, 2 * g + c + 1 + 8 * it)
                    nc.vector.tensor_tensor(w_lo[:, g % SLOTS, part], raw[:, g % RAW_SLOTS, part],
                                            w_hi[:, g % SLOTS, part].bitcast(F32), ALU.subtract).then_inc(lo_ready, 1)

            def y_low(b, d):
                t0 = SUBS[b].t_in
                v.wait_ge(yh_ready, KT * b + d + 1)
                nc.vector.scalar_tensor_tensor(
                    out=y_lo[:, d, t0:L], in0=xT[:, d, t0:L],
                    scalar=gains[:, SUBS[b].pre + d:SUBS[b].pre + d + 1],
                    in1=y_hi[:, d, t0:L].bitcast(F32), op0=ALU.mult, op1=ALU.subtract).then_inc(yl_ready, 1)

            def pre_norm(b):
                t = SUBS[b]
                t0 = t.t_in
                v.wait_ge(x_sq, 2 * b + 2)
                for n, m in enumerate((4, 2, 1)):
                    nc.vector.tensor_tensor(fT[:, 0:m, t0:L], fT[:, 0:m, t0:L], fT[:, m:2 * m, t0:L],
                                            ALU.add).then_inc(x_acc, 1)
                    v.wait_ge(x_acc, 3 * b + n + 1)
                conv_lo(t.g0 + 3)
                v.wait_ge(pre_sum, b + 1)
                nc.vector.tensor_scalar(pre_ms[:, t0:L], ps[:, BANK_PRE, t0:L], 1.0 / D, EPS,
                                        ALU.mult, ALU.add).then_inc(pre_var, 1)
                v.wait_ge(pre_var, b + 1)
                nc.vector.tensor_scalar(eps_ms[:, t0:L], pre_ms[:, t0:L], EPS, None, ALU.mult).then_inc(eps_ready, 1)
                v.wait_ge(eps_ready, b + 1)
                v.wait_ge(rms_ready, b + 1)

            for d in range(KT):
                v.wait_ge(x_turned, d + 1)
                nc.vector.tensor_copy(xT[:, d, :], ps[:, d, 0:L]).then_inc(x_ready, 1)
                if d == 0:
                    v.wait_ge(small_ready, 2)
                else:
                    y_low(0, d - 1)
                if d == 4:
                    conv_lo(0)
            y_low(0, KT - 1)
            conv_lo(1)
            conv_lo(2)
            pre_norm(0)

            for t in SUBS:
                if t.kind == "ffn":
                    base = pairs_before[t.u]
                    t0 = t.t_in

                    def in_step(i, it):
                        j = i // 2
                        b0 = BANK_IN[i % 4][0]
                        v.wait_ge(panel_done, t.g0 + i + 1 + 4 * it)
                        if i % 2 == 0:
                            nc.vector.tensor_tensor(act[:, j % 2, :, t0:L], ps[:, b0:b0 + 2, t0:L],
                                                    spread(rms_inv, 2, t0), ALU.mult).then_inc(gate_ready, 1)
                            conv_lo(t.g0 + i + 4, it)
                        else:
                            v.wait_ge(silu_ready, base + j + 1 + 2 * it)
                            nc.vector.tensor_tensor(hid[:, j % 2, :, t0:L], act[:, j % 2, :, t0:L],
                                                    ps[:, b0:b0 + 2, t0:L], ALU.mult).then_inc(h_ready, 1)
                            conv_lo(t.g0 + i + 4, it)
                            v.wait_ge(hh_ready, base + j + 1 + 2 * it)
                            nc.vector.tensor_tensor(h_lo[:, bass.ds(2 * j + 4 * it, 2), t0:L],
                                                    hid[:, j % 2, :, t0:L],
                                                    h_hi[:, bass.ds(2 * j + 4 * it, 2), t0:L].bitcast(F32),
                                                    ALU.subtract).then_inc(hl_ready, 1)
                            v.wait_ge(hl_ready, base + j + 1 + 2 * it)
                    steps(v, 22, in_step)
                else:
                    def drain(i, it):
                        b0 = BANK_IN[i % 4][0]
                        v.wait_ge(panel_done, t.g0 + i + 1 + 4 * it)
                        nc.vector.tensor_tensor(qkv[:, bass.ds(2 * i + 8 * it, 2), :], ps[:, b0:b0 + 2, 0:L],
                                                spread(rms_inv, 2, 0), ALU.mult).then_inc(proj_drained, 1)
                        conv_lo(t.g0 + i + 4, it)
                    steps(v, t.n_in, drain)
                if t.kind == "sb":
                    v.wait_ge(const_in_sem, 16)
                    for st in range(NH + 6):
                        if st == 2:
                            for n in range(1, 6, 2):
                                v.wait_ge(v_turned, n + 1)
                                nc.vector.tensor_copy(v_tok[:, n // 2, 512:1024], ps[:, 2 + n, :])\
                                    .then_inc(v_saved_d, 1)
                        if st < NH:
                            v.wait_ge(z_done, st + 1)
                            if st >= 4:
                                v.wait_ge(d_ready, st - 3)
                            nc.vector.scalar_tensor_tensor(out=z[:, st % 4], in0=ps[:, st % 2, 0:SB_W],
                                                           scalar=SCALE, in1=cst("mask_sb"), op0=ALU.mult,
                                                           op1=ALU.add).then_inc(z_ready, 1)
                            v.wait_ge(z_ready, st + 1)
                            if st >= 2:
                                v.wait_ge(sp_ready, st - 1)
                            nc.vector.scalar_tensor_tensor(out=e[:, st % 2], in0=z[:, st % 4], scalar=-1.0,
                                                           in1=z[:, st % 4], op0=ALU.mult,
                                                           op1=ALU.min).then_inc(e_abs, 1)
                        if 1 <= st < NH + 1:
                            h = st - 1
                            v.wait_ge(e_ln, h + 1)
                            if h >= 2:
                                v.wait_ge(c_done, h - 1)
                            nc.vector.scalar_tensor_tensor(out=sp[:, h % 2], in0=z[:, h % 4], scalar=0.0,
                                                           in1=e[:, h % 2], op0=ALU.max,
                                                           op1=ALU.add).then_inc(sp_ready, 1)
                        if 3 <= st < NH + 3:
                            h = st - 3
                            v.wait_ge(c_done, h + 1)
                            if h >= 3:
                                v.wait_ge(o_done, h - 2)
                            nc.vector.tensor_tensor(w[:, h % 3], z[:, h % 4], ps[:, 2 + h % 2, 0:SB_W],
                                                    ALU.subtract).then_inc(d_ready, 1)
                        if st >= 6 and (st - 6) % 2 == 0 and (st - 6) // 2 < 8:
                            q = (st - 6) // 2
                            v.wait_ge(oh_ready, q + 1)
                            nc.vector.tensor_tensor(y_lo[:, q, :], ps[:, 4 + q % 2, 0:L],
                                                    y_hi[:, q, :].bitcast(F32), ALU.subtract).then_inc(ol_ready, 1)
                elif t.kind == "swa":
                    for b in range(5):
                        b0 = BANK_IN[b % 4][0]
                        v.wait_ge(rot_done, b + 1)
                        if b >= 2:
                            v.wait_ge(roped, b - 1)
                        nc.vector.tensor_tensor(rot_s[:, b % 2], ps[:, b0:b0 + 2, 0:L], spread(cst("sin"), 2, 0),
                                                ALU.mult).then_inc(rs_ready, 1)
                        v.wait_ge(rs_ready, b + 1)
                        v.wait_ge(rc_ready, b + 1)
                        if b < 4:
                            nc.vector.tensor_tensor(qkv[:, 2 * b:2 * b + 2, :], rot_s[:, b % 2], rot_c[:, b % 2],
                                                    ALU.add).then_inc(roped, 1)
                        else:
                            for kv in range(NKV):
                                r = slice(HD * (kv % 2), HD * (kv % 2) + HD)
                                for to in range(2):
                                    nc.vector.tensor_tensor(kd[HD * to:HD * to + HD, kv, :],
                                                            rot_s[r, b % 2, kv // 2, :],
                                                            rot_c[r, b % 2, kv // 2, :], ALU.add).then_inc(roped, 1)
                    v.wait_ge(v_turned, 8)
                    nc.vector.tensor_copy(vt[0:META, 2, :], ps[0:META, 5, 0:NKV * HD]).then_inc(v_saved_d, 1)

                    def mask_scores(h):
                        gq = h // GROUP
                        v.wait_ge(s_done, h + 1)
                        if gq >= 2:
                            v.wait_ge(pt_done, h - 2 * GROUP + 1)
                        nc.vector.scalar_tensor_tensor(out=s[:, gq % 2, h % GROUP], in0=ps[:, h % 2, 0:SW_W],
                                                       scalar=SCALE, in1=cst("mask_sw"), op0=ALU.mult,
                                                       op1=ALU.add).then_inc(s_ready, 1)

                    def maxima(gq):
                        q = gq % 2
                        v.wait_ge(s_ready, GROUP * gq + GROUP)
                        for c in range(2):
                            nc.vector.tensor_reduce(top[:, q, c, :], s[:, q, :, SW_COL[c]:SW_COL[c] + SW_KEYS[c]],
                                                    AX.X, ALU.max).then_inc(stat, 1)
                        v.wait_ge(stat, 6 * gq + 2)
                        sk = sinks[:, GROUP * gq:GROUP * gq + GROUP].unsqueeze(1).broadcast_to([P, 2, GROUP])
                        nc.vector.tensor_tensor(top[:, q], top[:, q], sk, ALU.max).then_inc(stat, 1)
                        v.wait_ge(stat, 6 * gq + 3)
                        nc.vector.tensor_scalar(neg[:, q], top[:, q], -1.0, None, ALU.mult).then_inc(top_ready, 1)
                        v.wait_ge(top_ready, gq + 1)
                        nc.vector.tensor_tensor(snk[:, q], neg[:, q], sk, ALU.add).then_inc(snk_sum, 1)

                    def normalise(gq):
                        q = gq % 2
                        v.wait_ge(snk_exp, gq + 1)
                        v.wait_ge(p_exp, 8 * gq + 8)
                        nc.vector.tensor_tensor(den[:, q], tot[:, q], snk[:, q], ALU.add).then_inc(stat, 1)
                        v.wait_ge(stat, 6 * gq + 4)
                        nc.vector.reciprocal(inv[:, q], den[:, q]).then_inc(stat, 2)
                        v.wait_ge(stat, 6 * gq + 6)
                        for h in range(GROUP):
                            for c in range(2):
                                k0, k1 = SW_COL[c], SW_COL[c] + SW_KEYS[c]
                                nc.vector.tensor_scalar(s[:, q, h, k0:k1], s[:, q, h, k0:k1],
                                                        inv[:, q, c, h:h + 1], None, ALU.mult).then_inc(p_ready, 1)

                    def save_pt16(h):
                        v.wait_ge(pt_done, h + 1)
                        if h >= 2:
                            v.wait_ge(o_done, NH + h - 1)
                        nc.vector.tensor_copy(p_t16[:, h % 2], ps[0:META, 6 + h % 2, 0:256])\
                            .then_inc(pt16_saved, 1)

                    def save_o(q):
                        v.wait_ge(oh_ready, 8 + q + 1)
                        nc.vector.tensor_tensor(y_lo[:, q, META:L], ps[:, 2 + q % 2, 0:256],
                                                y_hi[:, q, META:L].bitcast(F32), ALU.subtract).then_inc(ol_ready, 1)
                    for h in range(GROUP):
                        mask_scores(h)
                    maxima(0)
                    for gq in range(NKV):
                        if gq + 1 < NKV:
                            for h in range(GROUP * gq + GROUP, GROUP * gq + 2 * GROUP):
                                mask_scores(h)
                        normalise(gq)
                        if gq + 1 < NKV:
                            maxima(gq + 1)
                        for h in range(GROUP * gq, GROUP * gq + GROUP):
                            save_pt16(h)
                            if h % 2 == 0 and h >= 2:
                                save_o(h // 2 - 1)
                    save_o(NH // 2 - 1)

                steps(v, n_split(t), lambda i, it: conv_lo(t.g_out + i + 4, it))
                k, t0 = t.u, t.t_out
                v.wait_ge(f_sq, 5 * k + 2)
                nc.vector.tensor_tensor(sq[:, 0:2, t0:L], sq[:, 0:2, t0:L], sq[:, 2:4, t0:L],
                                        ALU.add).then_inc(f_acc, 1)
                v.wait_ge(f_acc, 2 * k + 1)
                nc.vector.tensor_tensor(sq[:, 0, t0:L], sq[:, 0, t0:L], sq[:, 1, t0:L], ALU.add).then_inc(f_acc, 1)
                for d in range(6, 8):
                    v.wait_ge(f_sq, 5 * k + d - 2)
                    nc.vector.tensor_copy(fT[:, d, t0:L], ps[:, BANK_OUT[d], t0:L]).then_inc(f_saved2, 1)
                v.wait_ge(post_sum, k + 1)
                if t.kind == "ffn":
                    nc.vector.scalar_tensor_tensor(out=post_ms[:, t0:L], in0=ps[:, BANK_POST, t0:L],
                                                   scalar=1.0 / D, in1=eps_ms[:, t0:L], op0=ALU.mult,
                                                   op1=ALU.add).then_inc(post_var, 1)
                else:
                    nc.vector.tensor_scalar(post_ms[:, t0:L], ps[:, BANK_POST, t0:L], 1.0 / D, EPS,
                                            ALU.mult, ALU.add).then_inc(post_var, 1)
                v.wait_ge(post_ready, k + 1)
                v.wait_ge(f_saved, 3 * k + 3)
                v.wait_ge(f_saved2, 2 * k + 2)

                def u_of(d):
                    if d < KT:
                        if d >= 2:
                            v.wait_ge(x_ready, KT * (k + 1) + d - 1)
                        nc.vector.tensor_tensor(scaled[:, d % 2, t0:L], fT[:, d, t0:L], post_f[:, t0:L],
                                                ALU.mult).then_inc(u_ready, 1)

                u_of(0)
                for d in range(KT):
                    u_of(d + 1)
                    v.wait_ge(u_ready, KT * k + d + 1)
                    nc.vector.scalar_tensor_tensor(out=xT[:, d, t0:L], in0=scaled[:, d % 2, t0:L],
                                                   scalar=gains[:, t.post + d:t.post + d + 1],
                                                   in1=xT[:, d, t0:L], op0=ALU.mult,
                                                   op1=ALU.add).then_inc(x_ready, 1)
                    if t.u < 5 and d >= 1:
                        y_low(t.u + 1, d - 1)
                if t.u < 5:
                    y_low(t.u + 1, KT - 1)
                    pre_norm(t.u + 1)
                else:
                    for n in range(1, 4, 2):
                        v.wait_ge(out_turned, n + 1)
                        nc.vector.tensor_copy(x_rows(sq)[:, n // 2, 512:1024], ps[:, n, :]).then_inc(out_d, 1)

        @block.tensor
        def _(pe):
            def three(dst, slot, col, yh, yl, first, last):
                pc = slice(col, col + P)
                nc.tensor.matmul(dst, w_lo[:, slot, pc], yh, start=first, stop=False)
                nc.tensor.matmul(dst, w_hi[:, slot, pc], yh, start=False, stop=False)
                return nc.tensor.matmul(dst, w_hi[:, slot, pc], yl, start=False, stop=last)

            pe.wait_ge(few_landed, 16)
            pe.wait_ge(small_landed, 32)
            nc.tensor.transpose(ps[:, 0, 288:288 + 96], g_rows[:], cst("ident", 96, 0, 96))
            nc.tensor.matmul(ps[:, 1, 288:288 + NH], cst("ones", 1), s_row[:], start=True, stop=True)\
                .then_inc(small_T, 1)
            pe.wait_ge(x_landed, 32)
            pe.wait_ge(small_ready, 2)
            for d in range(KT):
                nc.tensor.transpose(ps[:, d, 0:META], meta_rows(fT)[:, P * d:P * d + P], cst("ident", META, 0, META))
                for c in range(2):
                    mm = nc.tensor.transpose(ps[:, d, META + P * c:META + P * c + P],
                                             x_rows(sq)[:, c, P * d:P * d + P], cst("ident"))
                mm.then_inc(x_turned, 1)

            for t in SUBS:
                t0 = t.t_in
                head = HEAD if t.u else 1
                for k in range(KT):
                    if k == KT - 1 and t.u:
                        pe.wait_ge(x_acc, 3 * t.u + 3)
                        nc.tensor.matmul(ps[:, BANK_PRE, t0:L], cst("ones"), fT[:, 0, t0:L],
                                         start=True, stop=True).then_inc(pre_sum, 1)
                    pe.wait_ge(yh_ready, KT * t.u + k + 1)
                    if k < KT - 1:
                        for i in range(head):
                            g = t.g0 + i
                            if k in (0, 4):
                                pe.wait_ge(lo_ready, 2 * g + 1 + k // 4)
                            for c in range(2):
                                dst = ps[:, BANK_IN[i][c], t0:L]
                                pc = slice(256 * k + P * c, 256 * k + P * c + P)
                                nc.tensor.matmul(dst, w_lo[:, g % SLOTS, pc], y_hi[:, k, t0:L],
                                                 start=(k == 0), stop=False)
                                nc.tensor.matmul(dst, w_hi[:, g % SLOTS, pc], y_hi[:, k, t0:L],
                                                 start=False, stop=False)
                        pe.wait_ge(yl_ready, KT * t.u + k + 1)
                        for i in range(head):
                            g = t.g0 + i
                            for c in range(2):
                                pc = slice(256 * k + P * c, 256 * k + P * c + P)
                                nc.tensor.matmul(ps[:, BANK_IN[i][c], t0:L], w_hi[:, g % SLOTS, pc],
                                                 y_lo[:, k, t0:L], start=False, stop=False)
                    else:
                        pe.wait_ge(yl_ready, KT * t.u + k + 1)
                        for i in range(head):
                            g = t.g0 + i
                            for c in range(2):
                                mm = three(ps[:, BANK_IN[i][c], t0:L], g % SLOTS, 256 * k + P * c,
                                           y_hi[:, k, t0:L], y_lo[:, k, t0:L], False, True)
                            mm.then_inc(panel_done, 1)

                def in_panel(i, it):
                    g = t.g0 + i
                    pe.wait_ge(lo_ready, 2 * g + 2 + 8 * it)
                    if i < 3:
                        pass
                    elif i == 3:
                        pe.wait_ge(pre_var, t.u + 1)
                    elif t.kind == "ffn":
                        done, n = (gate_ready, h_ready)[i % 2], pairs_before[t.u] + (i - 4) // 2 + 1
                        pe.wait_ge(done, n + 2 * it)
                    else:
                        pe.wait_ge(proj_drained, drained_before[t.u] + i - 3 + 4 * it)
                    for c in range(2):
                        for k in range(KT):
                            mm = three(ps[:, BANK_IN[i % 4][c], t0:L], g % SLOTS, 256 * k + P * c,
                                       y_hi[:, k, t0:L], y_lo[:, k, t0:L], k == 0, k == KT - 1)
                    mm.then_inc(panel_done, 1)

                for i in range(head, 3):
                    in_panel(i, 0)
                if t.u == 0:
                    pe.wait_ge(x_acc, 3)
                    nc.tensor.matmul(ps[:, BANK_PRE, t0:L], cst("ones"), fT[:, 0, t0:L],
                                     start=True, stop=True).then_inc(pre_sum, 1)
                in_panel(3, 0)
                steps(pe, t.n_in - 4, lambda i, it: in_panel(i + 4, it))

                if t.kind == "sb":
                    qd = drained_before[t.u]

                    def scores(h):
                        r = slice(HD * (h % 2), HD * (h % 2) + HD)
                        if h >= 2:
                            pe.wait_ge(z_ready, h - 1)
                        for n in range(3):
                            q0, k0 = SB_Q0[n], SB_KEY[n]
                            mm = nc.tensor.matmul(ps[:, h % 2, SB_COL[n]:SB_COL[n] + L - q0],
                                                  qkv[r, KT + h // 2, k0:k0 + P], qkv[r, h // 2, q0:L],
                                                  start=True, stop=True)
                        mm.then_inc(z_done, 1)

                    def running_sums(h):
                        pe.wait_ge(sp_ready, h + 1)
                        if h >= 2:
                            pe.wait_ge(d_ready, h - 1)
                        else:
                            pe.wait_ge(v_saved_a, 1)
                            pe.wait_ge(v_saved_d, 1)
                        for n in range(3):
                            for m in range(n, 3):
                                width = L - SB_Q0[m]
                                at = SB_COL[n] + SB_Q0[m] - SB_Q0[n]
                                mm = nc.tensor.matmul(ps[:, 2 + h % 2, at:at + width],
                                                      cst("tri" if m == n else "ones"),
                                                      sp[:, h % 2, SB_COL[m]:SB_COL[m] + width],
                                                      start=(m == n), stop=(m == 2), skip_group_check=True)
                        mm.then_inc(c_done, 1)

                    def values(h):
                        pe.wait_ge(w_ready, h + 1)
                        q = h // 2
                        if h == 0:
                            pe.wait_ge(v_saved_a, 3)
                            pe.wait_ge(v_saved_d, 3)
                        if q >= 2:
                            pe.wait_ge(ol_ready, q - 1)
                        r = slice(HD * (h % 2), HD * (h % 2) + HD)
                        for n in range(3):
                            mm = nc.tensor.matmul(ps[r, 4 + q % 2, SB_Q0[n]:L], v_tok[:, n, HD * h:HD * h + HD],
                                                  w[:, h % 3, SB_COL[n]:SB_COL[n] + L - SB_Q0[n]],
                                                  start=(n == 0), stop=(n == 2), skip_group_check=True)
                        mm.then_inc(o_done, 1)

                    pe.wait_ge(const_in_sem, 16)
                    pe.wait_ge(proj_drained, qd + 12)
                    scores(0)
                    scores(1)
                    for n in range(6):
                        for c in range(4):
                            mm = nc.tensor.transpose(
                                ps[:, 2 + n, P * c:P * c + P],
                                qkv[:, 2 * KT + 4 * (n % 2) + c, SB_KEY[n // 2]:SB_KEY[n // 2] + P], cst("ident"))
                        mm.then_inc(v_turned, 1)
                    for st in range(2, NH + 4):
                        if st < NH:
                            scores(st)
                        if 2 <= st < NH + 2:
                            running_sums(st - 2)
                        if 4 <= st:
                            values(st - 4)
                elif t.kind == "swa":
                    qd = drained_before[t.u]
                    for b in range(5):
                        if b == 0:
                            pe.wait_ge(proj_drained, qd + 5)
                        if b == 1:
                            pe.wait_ge(proj_drained, qd + 6)
                        if b == 4:
                            pe.wait_ge(rs_ready, 1)
                        for c in range(2):
                            mm = nc.tensor.matmul(ps[:, BANK_IN[b % 4][c], 0:L], cst("rot"), qkv[:, 2 * b + c, :],
                                                  start=True, stop=True)
                        mm.then_inc(rot_done, 1)
                    pe.wait_ge(rs_ready, 4)
                    for n in range(3):
                        rows = META if n == 2 else P
                        for c in range(2):
                            dst = ps[0:rows, 5, P * c:P * c + P] if n == 2 else \
                                ps[:, 6, 256 * n + P * c:256 * n + P * c + P]
                            mm = nc.tensor.transpose(dst, qkv[:, 10 + c, P * n:P * n + rows], cst("ident"))
                        if n:
                            mm.then_inc(v_turned, 1)

                    def scores(h):
                        r = slice(HD * (h % 2), HD * (h % 2) + HD)
                        kv = h // GROUP
                        if h >= 2:
                            pe.wait_ge(s_ready, h - 1)
                        for c in range(2):
                            mm = nc.tensor.matmul(ps[:, h % 2, SW_COL[c]:SW_COL[c] + SW_KEYS[c]],
                                                  qkv[r, h // 2, META + P * c:META + P * c + P],
                                                  kd[r, kv, 0:SW_KEYS[c]], start=True, stop=True)
                        mm.then_inc(s_done, 1)

                    def turn(h):
                        pr = s[:, (h // GROUP) % 2, h % GROUP]
                        pe.wait_ge(p_ready, 2 * h + 2)
                        if h >= 2:
                            pe.wait_ge(pt_saved, h - 1)
                            pe.wait_ge(pt16_saved, h - 1)
                        b = 4 + h % 2
                        c1 = SW_COL[1]
                        nc.tensor.transpose(ps[:, b, 0:P], pr[:, 0:P], cst("ident"))
                        nc.tensor.transpose(ps[:, b, P:2 * P], pr[:, c1:c1 + P], cst("ident"))
                        nc.tensor.transpose(ps[:, b, 2 * P:3 * P], pr[:, c1 + P:c1 + 2 * P], cst("ident"))
                        nc.tensor.transpose(ps[0:META, 6 + h % 2, 0:P], pr[:, P:P + META], cst("ident"))
                        nc.tensor.transpose(ps[0:META, 6 + h % 2, P:2 * P], pr[:, c1 + 2 * P:c1 + 2 * P + META],
                                            cst("ident")).then_inc(pt_done, 1)

                    def values(h):
                        q = h // 2
                        r = slice(HD * (h % 2), HD * (h % 2) + HD)
                        vc = slice(HD * (h // GROUP), HD * (h // GROUP) + HD)
                        pe.wait_ge(pt_saved, h + 1)
                        pe.wait_ge(pt16_saved, h + 1)
                        if q >= 2:
                            pe.wait_ge(ol_ready, 8 + q - 1)
                        big, small = p_t[:, h % 2], p_t16[:, h % 2]
                        mv = nc.tensor.matmul
                        d0, d1 = ps[r, 2 + q % 2, 0:P], ps[r, 2 + q % 2, P:2 * P]
                        mv(d0, vt[:, 0, vc], big[:, 0:P], start=True, stop=False)
                        mv(d0, vt[0:META, 1, vc], small[:, 0:P], start=False, stop=True)
                        mv(d1, vt[:, 0, vc], big[:, P:2 * P], start=True, stop=False)
                        mv(d1, vt[:, 1, vc], big[:, 2 * P:3 * P], start=False, stop=False)
                        mv(d1, vt[0:META, 2, vc], small[:, P:2 * P], start=False, stop=True).then_inc(o_done, 1)

                    pe.wait_ge(roped, 4 + 8)
                    pe.wait_ge(rs_ready, 5)
                    for h in range(GROUP):
                        scores(h)
                    pe.wait_ge(v_saved_a, 4)
                    pe.wait_ge(v_saved_d, 4)
                    for gq in range(NKV):
                        if gq + 1 < NKV:
                            for h in range(GROUP * gq + GROUP, GROUP * gq + 2 * GROUP):
                                scores(h)
                        for h in range(GROUP * gq, GROUP * gq + GROUP):
                            turn(h)
                            if h:
                                values(h - 1)
                    values(NH - 1)

                t0 = t.t_out
                src_hi, src_lo = (h_hi, h_lo) if t.kind == "ffn" else (y_hi, y_lo)

                def out_panel(i, it, first=False, last=False):
                    g = t.g_out + i
                    pe.wait_ge(lo_ready, 2 * g + 2 + 8 * it)
                    if t.kind == "ffn":
                        pe.wait_ge(hl_ready, pairs_before[t.u] + i + 1 + 4 * it)
                    elif first:
                        pe.wait_ge(ol_ready, 8 if t.kind == "sb" else 16)
                    for d in range(KT):
                        if first and t.kind == "ffn" and d % 2 == 0:
                            pe.wait_ge((gate_ready, h_ready)[d // 2 % 2], pairs_before[t.u] + 10 + d // 4)
                        for c in range(2):
                            mm = three(ps[:, BANK_OUT[d], t0:L], g % SLOTS, D * c + P * d,
                                       src_hi[:, 2 * i + c + 8 * it, t0:L], src_lo[:, 2 * i + c + 8 * it, t0:L],
                                       first and c == 0, last and c == 1)
                        if last:
                            mm.then_inc(f_done, 1)
                            if d == 6:
                                post_sums(0, 4)
                    if last:
                        post_sums(5, 6, 7)
                    else:
                        mm.then_inc(panel_done, 1)

                def post_sums(*tiles):
                    for d in tiles:
                        if d == 0:
                            pe.wait_ge(f_acc, 2 * t.u + 2)
                            pe.wait_ge(f_saved, 3 * t.u + 2)
                        else:
                            pe.wait_ge(f_sq, 5 * t.u + (3 if d < 6 else d - 2))
                        mm = nc.tensor.matmul(ps[:, BANK_POST, t0:L], cst("ones"), sq[:, d, t0:L],
                                              start=(d == 0), stop=(d == 7))
                        if d == 5:
                            mm.then_inc(panel_done, 1)
                    if d == 7:
                        mm.then_inc(post_sum, 1)

                out_panel(0, 0, first=True)
                steps(pe, t.n_out - 2, lambda i, it: out_panel(i + 1, it))
                out_panel(t.n_out - 1, 0, last=True)
            for n in range(4):
                for c in range(4):
                    d = 4 * (n % 2) + c
                    pe.wait_ge(x_ready, KT * 6 + d + 1)
                    mm = nc.tensor.transpose(ps[:, n, P * c:P * c + P],
                                             xT[:, d, META + P * (n // 2):META + P * (n // 2) + P], cst("ident"))
                mm.then_inc(out_turned, 1)


_INS = ["x", "meta_tokens", "norm_g", "ffn_w_gate", "ffn_w_up", "ffn_w_down", "sb_w_in", "sb_w_out",
        "swa_w_in", "swa_sinks", "swa_w_out"]


def constants():
    c = np.zeros((P, CONST_W), np.float32)

    def part(name):
        lo, hi = CONST[name]
        return c[:, lo:hi]

    p = np.arange(P)
    for n in range(3):
        q = np.arange(SB_Q0[n], L)
        key = SB_KEY[n] + p
        seen = (key[:, None] < q[None, :]) & (key[:, None] >= (256 if n == 2 else 0))
        part("mask_sb")[:, SB_COL[n]:SB_COL[n] + len(q)] = np.where(seen, 0, HIDDEN)
    part("tri")[:] = p[:, None] >= p[None, :]
    part("ident")[:] = np.eye(P)
    part("ones")[:] = 1
    for n in range(2):
        key = np.arange(SW_KEYS[n])
        key_chunk = np.where(key < META, -1, (key - META) // CHUNK)
        own = (2 * n + p // CHUNK)[:, None]
        seen = (key_chunk == -1) | ((key_chunk >= own - 1) & (key_chunk <= own))
        part("mask_sw")[:, SW_COL[n]:SW_COL[n] + len(key)] = np.where(seen, 0, HIDDEN)
    first = p % HD < HD // 2
    part("rot")[np.where(first, p + HD // 2, p - HD // 2), p] = np.where(first, -1, 1)
    freq = np.float32(THETA) ** (-np.arange(HD // 2, dtype=np.float32) / np.float32(HD // 2))
    angle = np.arange(L, dtype=np.float32)[None, :] * freq[p % (HD // 2)][:, None]
    part("cos")[:] = np.cos(angle)
    part("sin")[:] = np.sin(angle)
    return c


def kernel(**inputs):
    import numpy as _np
    import concourse.bacc as _bacc
    from concourse import mybir as _mybir
    from concourse.bass_utils import run_bass_kernel_spmd as _run

    nc = _bacc.Bacc("TRN2", target_bir_lowering=False, num_devices=1)
    arrays, args = {}, []
    for name in _INS:
        a = _np.ascontiguousarray(inputs[name])
        arrays[f"in_{name}_dram"] = a
        args.append(nc.dram_tensor(f"in_{name}_dram", a.shape, _mybir.dt.from_np(a.dtype), kind="ExternalInput").ap())
    c = constants()
    arrays["const_dram"] = c
    args.append(nc.dram_tensor("const_dram", c.shape, F32, kind="ExternalInput").ap())
    args.append(nc.dram_tensor("out_0_dram", (1, SEQ, D), F32, kind="ExternalOutput").ap())
    x, *rest, out = args
    build(nc, x.rearrange("b s d -> (b s) d"), *rest, out.rearrange("b s d -> (b s) d"))
    r = _run(nc, [arrays], core_ids=[0])
    return r.results[0]["out_0_dram"]
```

```python
from contextlib import ExitStack

import numpy as np

import concourse.bass as bass
from concourse import mybir

P = 128
D = 1024
KT = D // P
SEQ = 256
META = 16
L = META + SEQ
DEPTH = 2
FF = 2816
HD = 64
NH = D // HD
NKV = 4
GROUP = NH // NKV
CHUNK = 64
THETA = 10000.0
EPS = 1e-6
SCALE = HD ** -0.5
HIDDEN = -1e30

PW = 2048
RAW_SLOTS = 2
SLOTS = 4
HALF = PW // 2

SB_KEY = [0, 128, L - P]
SB_Q0 = [0, 128, 256]
SB_COL = [16, 288, 0]
SB_W = 432
SB_PAD = P - 16
SW_TOKENS = [list(range(144)), list(range(META)) + list(range(80, L))]
SW_RUNS = [(0, 0, 144), (144, 0, META), (160, 80, 192)]
SW_KEYS = [len(t) for t in SW_TOKENS]
SW_COL = [0, 144]
SW_W = 352
SW_WIN = [(0, 0, 0), (0, 16, 112), (1, 0, 0), (1, 80, 48)]
SWA_PANELS = [4, 0, 1, 2, 3, 5]
SW_EXP, SW_LAG = 5, 8

CONST = {}
_at = 0
for _n, _w in (("ident", P), ("ones", P), ("mask_sb", SB_W), ("tri", P), ("mask_sw", SW_W),
               ("rot", P), ("cos", L), ("sin", L)):
    CONST[_n] = (_at, _at + _w)
    _at += _w
CONST_W = _at
FEW = 2 * P

F32 = mybir.dt.float32
F32R = mybir.dt.float32r
ALU = mybir.AluOpType
ACT = mybir.ActivationFunctionType
AX = mybir.AxisListType


class Sub:

    def __init__(self, u, kind, g0, n_in, n_out, t_in, t_out):
        self.u, self.kind, self.g0, self.n_in, self.n_out = u, kind, g0, n_in, n_out
        self.layer, self.part = u // 3, u % 3
        self.pre = (self.layer * 6 + 2 * self.part) * KT
        self.post = self.pre + KT
        self.t_in, self.t_out = t_in, t_out
        self.factor = 1.0 if self.part == 1 else 0.5
        self.g_out = g0 + n_in
        self.end = g0 + n_in + n_out


def plan():
    subs, g = [], 0
    for u, (kind, n_in, n_out) in enumerate([("ffn", 22, 11), ("sb", 12, 4), ("ffn", 22, 11),
                                             ("ffn", 22, 11), ("swa", 6, 4), ("ffn", 22, 11)]):
        subs.append(Sub(u, kind, g, n_in, n_out, META if u == 5 else 0, META if u >= 4 else 0))
        g += n_in + n_out
    return subs, g


SUBS, PANELS = plan()
BANK_IN = [(0, 1), (2, 3), (4, 5), (6, 7)]
BANK_OUT = [4, 5, 6, 7, 0, 1, 2, 3]
BANK_POST, BANK_PRE = 6, 7
ROT_BANK = [4, 6, 4, 6, 4]
ROPE_AT = {4: 3, 6: 4}
OUT_PARTS = [(0, 0), (1, 0), (0, 1), (1, 1)]
HEAD = 3


def build(nc, x_in, meta_in, norm_g, w_gate, w_up, w_down, sb_w_in, sb_w_out,
          swa_w_in, swa_sinks, swa_w_out, const_in, out):
    ctx = ExitStack()
    with ctx:
        def sb(name, shape, dt=F32):
            return ctx.enter_context(nc.sbuf_tensor(name, shape, dt))

        def sem(name):
            return ctx.enter_context(nc.semaphore(name))

        ps = ctx.enter_context(nc.psum_tensor("ps", [P, 8, 512], F32))
        const = sb("const", [P, CONST_W])
        raw = sb("raw", [P, RAW_SLOTS, PW])
        w_hi = sb("w_hi", [P, SLOTS, PW], F32R)
        w_lo = sb("w_lo", [P, SLOTS, PW], F32R)
        xT = sb("xT", [P, KT, L])
        y_hi = sb("y_hi", [P, KT, L], F32R)
        y_lo = sb("y_lo", [P, KT, L], F32R)
        fT = sb("fT", [P, KT, L])
        sq = sb("sq", [P, KT, L])
        gains = sb("gains", [P, DEPTH * 6 * KT])
        sinks = sb("sinks", [P, NH])
        rms_inv = sb("rms_inv", [P, L])
        pre_ms = sb("pre_ms", [P, L])
        pre_ln = sb("pre_ln", [P, L])
        eps_ms = sb("eps_ms", [P, L])
        post_ln = sb("post_ln", [P, L])
        post_f = sb("post_f", [P, L])
        scaled = sb("scaled", [P, 2, L])
        g_rows = sb("g_rows", [DEPTH * 6 * KT, P])
        s_row = sb("s_row", [1, NH])

        with ExitStack() as over:
            def ffn_sb(name, shape, dt=F32):
                return over.enter_context(nc.sbuf_tensor(name, shape, dt))
            h_hi = ffn_sb("h_hi", [P, FF // P, L], F32R)
            h_lo = ffn_sb("h_lo", [P, FF // P, L], F32R)
            act = ffn_sb("act", [P, 2, 2, L])
            hid = ffn_sb("hid", [P, 2, 2, L])
        with ExitStack() as over:
            def mix_sb(name, shape, dt=F32):
                return over.enter_context(nc.sbuf_tensor(name, shape, dt))
            qkv = mix_sb("qkv", [P, 3 * KT, L])
            v_tok = mix_sb("v_tok", [P, 3, D])
            z = mix_sb("z", [P, 4, SB_W])
            e = mix_sb("e", [P, 2, SB_W])
            sp = mix_sb("sp", [P, 2, SB_PAD + SB_W])
            w = mix_sb("w", [P, 3, SB_PAD + SB_W])
        with ExitStack() as over:
            def swa_sb(name, shape, dt=F32):
                return over.enter_context(nc.sbuf_tensor(name, shape, dt))
            swa_sb("under_qkv", [P, 12, L])
            kd = swa_sb("kd", [P, NKV, SW_W])
            v_win = swa_sb("v_win", [P, 2, 4, P])
            vt = swa_sb("vt", [P, 4, NKV * HD])
            rot_s = swa_sb("rot_s", [P, 2, L])
            rot_c = swa_sb("rot_c", [P, 2, L])
            s = swa_sb("s", [P, 3, GROUP, SW_W])
            p_t = swa_sb("p_t", [P, 2, 512])
            top = swa_sb("top", [P, 2, 2, GROUP])
            neg = swa_sb("neg", [P, 2, 2, GROUP])
            tot = swa_sb("tot", [P, 2, 2, GROUP])
            snk = swa_sb("snk", [P, 2, 2, GROUP])
            den = swa_sb("den", [P, 2, 2, GROUP])
            inv = swa_sb("inv", [P, 2, 2, GROUP])

        def cst(name, rows=P, a=0, b=None):
            lo, hi = CONST[name]
            return const[0:rows, lo + a:(hi if b is None else lo + b)]

        def spread(ap, n, t0):
            return ap[:, t0:L].unsqueeze(1).broadcast_to([P, n, L - t0])

        def x_rows(t):
            return t[:].rearrange("p a b -> p (a b)")[:, 0:2 * D].rearrange("p (a n) -> p a n", a=2)

        def meta_rows(t):
            return t[0:META].rearrange("p a b -> p (a b)")[:, 0:D]

        few_landed = sem("few_landed")
        const_in_sem = sem("const_landed")
        x_landed = sem("x_landed")
        small_landed = sem("small_landed")
        raw_landed = [sem(f"raw_landed{i}") for i in range(RAW_SLOTS)]
        hi_ready = sem("hi_ready")
        lo_ready = sem("lo_ready")
        panel_done = sem("panel_done")
        small_T = sem("small_T")
        small_ready = sem("small_ready")
        x_turned = sem("x_turned")
        gate_ready = sem("gate_ready")
        silu_ready = sem("silu_ready")
        h_ready = sem("h_ready")
        hh_ready = sem("hh_ready")
        hl_ready = sem("hl_ready")
        f_done = sem("f_done")
        f_sq = sem("f_sq")
        f_saved = sem("f_saved")
        f_saved2 = sem("f_saved2")
        f_acc = sem("f_acc")
        post_sum = sem("post_sum")
        post_log = sem("post_log")
        eps_ready = sem("eps_ready")
        post_ready = sem("post_ready")
        u_ready = sem("u_ready")
        x_ready = sem("x_ready")
        yh_ready = sem("yh_ready")
        yl_ready = sem("yl_ready")
        x_sq = sem("x_sq")
        x_acc = sem("x_acc")
        pre_sum = sem("pre_sum")
        pre_var = sem("pre_var")
        pre_log = sem("pre_log")
        rms_ready = sem("rms_ready")
        proj_drained = sem("proj_drained")
        v_turned = sem("v_turned")
        win_zero = sem("win_zero")
        win_ready = sem("win_ready")
        kd_ready = sem("kd_ready")
        v_saved_a = sem("v_saved_a")
        v_saved_d = sem("v_saved_d")
        pad_zero = sem("pad_zero")
        z_done = sem("z_done")
        z_ready = sem("z_ready")
        e_abs = sem("e_abs")
        e_exp = sem("e_exp")
        e_ln = sem("e_ln")
        sp_ready = sem("sp_ready")
        c_done = sem("c_done")
        d_ready = sem("d_ready")
        w_ready = sem("w_ready")
        o_done = sem("o_done")
        oh_ready = sem("oh_ready")
        ol_ready = sem("ol_ready")
        rot_done = sem("rot_done")
        rs_ready = sem("rs_ready")
        rc_ready = sem("rc_ready")
        roped = sem("roped")
        s_done = sem("s_done")
        s_ready = sem("s_ready")
        top_ready = sem("top_ready")
        p_exp = sem("p_exp")
        stat = sem("stat")
        den_ready = sem("den_ready")
        inv_ready = sem("inv_ready")
        snk_sum = sem("snk_sum")
        snk_exp = sem("snk_exp")
        p_ready = sem("p_ready")
        pt_done = sem("pt_done")
        pt_saved = sem("pt_saved")
        out_turned = sem("out_turned")
        out_a = sem("out_a")
        out_d = sem("out_d")
        out_stored = sem("out_stored")

        pairs_before = [11 * sum(1 for t in SUBS[:u] if t.kind == "ffn") for u in range(7)]
        drained_before = [sum(t.n_in for t in SUBS[:u] if t.kind != "ffn") for u in range(7)]

        def steps(eng, n, body):
            if n >= 8:
                with eng.Fori(0, n // 4) as it:
                    for i in range(4):
                        body(i, it)
                rest = range(n // 4 * 4, n)
            else:
                rest = range(n)
            for i in rest:
                body(i, 0)

        def n_split(t):
            return min(t.n_out - 1, PANELS - t.g_out - SLOTS)

        block = ctx.enter_context(nc.Block())

        @block.sync
        def _(sp_eng):
            sp_eng.dma_start(x_rows(sq), x_in.rearrange("(a p) d -> p a d", p=P)).then_inc(x_landed, 16)

            def load(g, more, src):
                if g >= RAW_SLOTS:
                    sp_eng.wait_ge(lo_ready, 2 * (g - RAW_SLOTS + 1) + 2 * more)
                sp_eng.dma_start(raw[:, g % RAW_SLOTS, :].rearrange("p (k n) -> p k n", n=src.shape[-1]), src)\
                      .then_inc(raw_landed[g % RAW_SLOTS], 16)

            def columns(wt, i):
                return wt.rearrange("(k p) n -> p k n", p=P)[:, :, bass.ds(256 * i, 256)]

            def rows(wt, i):
                return wt.rearrange("(r c p) n -> p r c n", c=2, p=P)[:, bass.ds(i, 1)].rearrange(
                    "p r c n -> p (r c) n")

            def pairs(lo, n, body):
                with sp_eng.Fori(0, n // 2) as it:
                    for c in range(2):
                        body(lo + c, 2 * it, 2 * it + c)
                if n % 2:
                    body(lo + n - 1, 0, n - 1)

            for t in SUBS:
                if t.kind == "ffn":
                    j = t.part // 2
                    if t.u == 0:
                        load(0, 0, columns(w_gate[0, 0], 0))
                        sp_eng.wait_ge(small_landed, 32)
                        load(1, 0, columns(w_up[0, 0], 0))
                        with sp_eng.Fori(1, 11) as it:
                            load(2, 2 * it - 2, columns(w_gate[0, 0], it))
                            load(3, 2 * it - 2, columns(w_up[0, 0], it))
                    else:
                        with sp_eng.Fori(0, 11) as it:
                            load(t.g0, 2 * it, columns(w_gate[t.layer, j], it))
                            load(t.g0 + 1, 2 * it, columns(w_up[t.layer, j], it))
                    pairs(t.g_out, 11, lambda g, more, i: load(g, more, rows(w_down[t.layer, j], i)))
                else:
                    w_in, w_out = (sb_w_in[0], sb_w_out[0]) if t.kind == "sb" else (swa_w_in[0], swa_w_out[0])
                    if t.kind == "sb":
                        pairs(t.g0, t.n_in, lambda g, more, i: load(g, more, columns(w_in, i)))
                    else:
                        for i in range(t.n_in):
                            load(t.g0 + i, 0, columns(w_in, SWA_PANELS[i]))
                    pairs(t.g_out, t.n_out, lambda g, more, i: load(g, more, rows(w_out, i)))

            out_v = out.rearrange("(a p) d -> a p d", p=P)
            for n, (a, half) in enumerate(OUT_PARTS):
                if n < 3:
                    sp_eng.wait_ge(out_a, n + 1)
                else:
                    sp_eng.wait_ge(out_d, 1)
                sp_eng.dma_start(out_v[a, :, 512 * half:512 * half + 512],
                                 x_rows(sq)[:, a, 512 * half:512 * half + 512]).then_inc(out_stored, 16)
            sp_eng.wait_ge(out_stored, 64)

        @block.gpsimd
        def _(pool):
            pool.wait_ge(proj_drained, 1)
            nc.gpsimd.memset(sp[:, :, 0:SB_PAD], 0.0).then_inc(pad_zero, 1)
            nc.gpsimd.memset(w[:, :, 0:SB_PAD], 0.0).then_inc(pad_zero, 1)
            pool.wait_ge(const_in_sem, 16)
            for b in range(5):
                pool.wait_ge(proj_drained, drained_before[4] + b + 1)
                if b == 0:
                    nc.gpsimd.memset(v_win[:], 0.0).then_inc(win_zero, 1)
                else:
                    pool.wait_ge(roped, b)
                nc.gpsimd.tensor_tensor(rot_c[:], qkv[:, 2 * b:2 * b + 2, :],
                                        spread(cst("cos"), 2, 0), ALU.mult).then_inc(rc_ready, 1)
                if b == 2:
                    pool.wait_ge(proj_drained, drained_before[4] + 6)
                    pool.wait_ge(win_zero, 1)
                    for n, (c, k0, zero) in enumerate(SW_WIN):
                        tokens = SW_TOKENS[c][k0 + zero:k0 + P]
                        cut = [i for i in range(len(tokens)) if i == 0 or tokens[i] != tokens[i - 1] + 1] + [len(tokens)]
                        for i0, i1 in zip(cut, cut[1:]):
                            cp = nc.gpsimd.tensor_copy(v_win[:, :, n, zero + i0:zero + i1],
                                                       qkv[:, 10:12, tokens[i0]:tokens[i0] + i1 - i0])
                        cp.then_inc(win_ready, 1)

        @block.scalar
        def _(a):
            def conv_hi(g, it=0):
                if g >= PANELS:
                    return
                a.wait_ge(raw_landed[g % RAW_SLOTS], 16 * (g // RAW_SLOTS + 1) + 32 * it)
                if g >= SLOTS:
                    a.wait_ge(panel_done, g - SLOTS + 1 + 4 * it)
                for c in range(2):
                    part = slice(c * HALF, (c + 1) * HALF)
                    nc.scalar.copy(w_hi[:, g % SLOTS, part], raw[:, g % RAW_SLOTS, part]).then_inc(hi_ready, 1)

            def split_y(b):
                t0 = SUBS[b].t_in
                for d in range(0 if b == 0 else 1, KT):
                    a.wait_ge(x_ready, KT * b + d + 1)
                    nc.scalar.activation(y_hi[:, d, t0:L], xT[:, d, t0:L], ACT.Copy,
                                         scale=gains[:, SUBS[b].pre + d:SUBS[b].pre + d + 1]).then_inc(yh_ready, 1)
                if b == 0:
                    a.dma_start(const[:, FEW:CONST_W], const_in[:, FEW:CONST_W]).then_inc(const_in_sem, 16)
                    conv_hi(1)
                    conv_hi(2)
                for c in range(2):
                    nc.scalar.activation(fT[:, 4 * c:4 * c + 4, t0:L], xT[:, 4 * c:4 * c + 4, t0:L],
                                         ACT.Square).then_inc(x_sq, 1)
                conv_hi(SUBS[b].g0 + 3)
                a.wait_ge(pre_var, b + 1)
                nc.scalar.activation(pre_ln[:, t0:L], pre_ms[:, t0:L], ACT.Ln).then_inc(pre_log, 1)
                a.wait_ge(pre_log, b + 1)
                nc.scalar.activation(rms_inv[:, t0:L], pre_ln[:, t0:L], ACT.Exp, scale=-0.5).then_inc(rms_ready, 1)
                if SUBS[b].kind == "ffn":
                    nc.scalar.preload_act_table_set("silu_and_others")

            a.dma_start(const[:, 0:FEW], const_in[:, 0:FEW]).then_inc(few_landed, 16)
            a.dma_start(meta_rows(fT), meta_in).then_inc(x_landed, 16)
            a.dma_start(g_rows[:], norm_g.rearrange("l n (k p) -> (l n k) p", p=P)).then_inc(small_landed, 16)
            a.dma_start(s_row[:], swa_sinks).then_inc(small_landed, 16)
            nc.scalar.preload_act_table_set("natural_log_exp_and_others")
            conv_hi(0)
            a.wait_ge(small_T, 1)
            nc.scalar.copy(gains[:], ps[:, 7, 288:288 + 96]).then_inc(small_ready, 1)
            nc.scalar.copy(sinks[:], ps[:, 7, 384:384 + NH]).then_inc(small_ready, 1)
            a.wait_ge(small_ready, 2)
            split_y(0)

            for t in SUBS:
                if t.kind == "ffn":
                    base = pairs_before[t.u]

                    def in_step(i, it):
                        conv_hi(t.g0 + i + 4, it)
                        j = i // 2
                        if i % 2 == 0:
                            a.wait_ge(gate_ready, base + j + 1 + 2 * it)
                            nc.scalar.activation(act[:, j % 2, :, t.t_in:L], act[:, j % 2, :, t.t_in:L],
                                                 ACT.Silu).then_inc(silu_ready, 1)
                        else:
                            a.wait_ge(h_ready, base + j + 1 + 2 * it)
                            nc.scalar.copy(h_hi[:, bass.ds(2 * j + 4 * it, 2), t.t_in:L],
                                           hid[:, j % 2, :, t.t_in:L]).then_inc(hh_ready, 1)
                    steps(a, 22, in_step)
                elif t.kind == "sb":
                    steps(a, 8, lambda i, it: conv_hi(t.g0 + i + 4, it))
                    for i in range(8, 11):
                        conv_hi(t.g0 + i + 4)
                    for n in range(0, 6, 2):
                        a.wait_ge(v_turned, n + 1)
                        nc.scalar.copy(v_tok[:, n // 2, 0:512], ps[:, 2 + n, :]).then_inc(v_saved_a, 1)
                    for st in range(NH + 5):
                        if st < NH:
                            a.wait_ge(e_abs, st + 1)
                            nc.scalar.activation(e[:, st % 2], e[:, st % 2], ACT.Exp).then_inc(e_exp, 1)
                        if 3 <= st < NH + 3:
                            h = st - 3
                            a.wait_ge(d_ready, h + 1)
                            nc.scalar.activation(w[:, h % 3, SB_PAD:], w[:, h % 3, SB_PAD:], ACT.Exp).then_inc(w_ready, 1)
                        if st < NH:
                            a.wait_ge(e_exp, st + 1)
                            nc.scalar.activation(e[:, st % 2], e[:, st % 2], ACT.Ln, bias=1.0).then_inc(e_ln, 1)
                        if st >= 5 and (st - 5) % 2 == 1:
                            q = (st - 5) // 2
                            a.wait_ge(o_done, 2 * q + 2)
                            nc.scalar.copy(y_hi[:, q, :], ps[:, 4 + q % 2, 0:L]).then_inc(oh_ready, 1)
                    conv_hi(t.g_out + 3)
                else:
                    for i in range(t.n_in):
                        if i < 4:
                            conv_hi(t.g0 + i + 4)
                        if i == 2:
                            a.wait_ge(roped, 1)
                            for half in range(2):
                                r = slice(HD * half, HD * half + HD)
                                for to in range(2):
                                    for at, tok, n in SW_RUNS:
                                        nc.scalar.copy(kd[HD * to:HD * to + HD, half:NKV:2, at:at + n],
                                                       qkv[r, 0:2, tok:tok + n]).then_inc(kd_ready, 1)
                    def exps(h):
                        gq, q = h // GROUP, h // GROUP % 2
                        if h % GROUP == 0:
                            a.wait_ge(snk_sum, gq + 1)
                            nc.scalar.activation(snk[:, q], snk[:, q], ACT.Exp).then_inc(snk_exp, 1)
                        for c in range(2):
                            k0, k1 = SW_COL[c], SW_COL[c] + SW_KEYS[c]
                            nc.scalar.activation(s[:, gq % 3, h % GROUP, k0:k1], s[:, gq % 3, h % GROUP, k0:k1],
                                                 ACT.Exp, bias=neg[:, q, c, h % GROUP:h % GROUP + 1],
                                                 accum_out=tot[:, q, c, h % GROUP:h % GROUP + 1]).then_inc(p_exp, 1)

                    def save_o(q):
                        a.wait_ge(o_done, NH + 2 * q + 2)
                        nc.scalar.copy(y_hi[:, q, META:L], ps[:, 6 + q % 2, 0:256]).then_inc(oh_ready, 1)

                    for st in range(NH + SW_LAG + 3):
                        h = st - SW_LAG
                        if 0 <= h < NH:
                            a.wait_ge(pt_done, h + 1)
                            if h >= 2:
                                a.wait_ge(o_done, NH + h - 1)
                            nc.scalar.copy(p_t[:, h % 2], ps[:, 4 + h % 2, :]).then_inc(pt_saved, 1)
                        if 0 <= st - SW_EXP < NH:
                            exps(st - SW_EXP)
                        if st == 6:
                            for n in range(2):
                                a.wait_ge(v_turned, 6 + n + 1)
                                nc.scalar.copy(vt[:, 2 * n:2 * n + 2, :],
                                               ps[:, 6 + n, :].rearrange("p (a b) -> p a b", a=2)).then_inc(v_saved_a, 1)
                        if h >= 3 and (h - 3) % 2 == 0 and (h - 3) // 2 < NH // 2:
                            save_o((h - 3) // 2)
                    conv_hi(t.g_out + 2)
                    conv_hi(t.g_out + 3)

                if t.kind == "ffn":
                    nc.scalar.preload_act_table_set("natural_log_exp_and_others")
                steps(a, n_split(t), lambda i, it: conv_hi(t.g_out + i + 4, it))
                k = t.u
                t0 = t.t_out
                def save_f(n):
                    b0 = BANK_OUT[2 * n]
                    nc.scalar.copy(fT[:, 2 * n:2 * n + 2, t0:L], ps[:, b0:b0 + 2, t0:L]).then_inc(f_saved, 1)

                for n in range(3):
                    a.wait_ge(f_done, KT * k + 2 * n + 2)
                    b0 = BANK_OUT[2 * n]
                    nc.scalar.activation(sq[:, 2 * n:2 * n + 2, t0:L], ps[:, b0:b0 + 2, t0:L], ACT.Square)\
                        .then_inc(f_sq, 1)
                    if n < 2:
                        save_f(n)
                for d in range(6, 8):
                    a.wait_ge(f_done, KT * k + d + 1)
                    nc.scalar.activation(sq[:, d, t0:L], ps[:, BANK_OUT[d], t0:L], ACT.Square).then_inc(f_sq, 1)
                save_f(2)
                a.wait_ge(post_sum, k + 1)
                nc.scalar.activation(post_ln[:, t0:L], ps[:, BANK_POST, t0:L], ACT.Ln,
                                     scale=t.factor ** -2 / D).then_inc(post_log, 1)
                a.wait_ge(post_log, k + 1)
                nc.scalar.activation(post_f[:, t0:L], post_ln[:, t0:L], ACT.Exp, scale=-0.5).then_inc(post_ready, 1)
                if t.u < 5:
                    split_y(t.u + 1)
                else:
                    for n, (c, half) in enumerate(OUT_PARTS[:3]):
                        a.wait_ge(out_turned, n + 1)
                        nc.scalar.copy(x_rows(sq)[:, c, 512 * half:512 * half + 512], ps[:, n, :]).then_inc(out_a, 1)

        @block.vector
        def _(v):
            def conv_lo(g, it=0):
                if g >= PANELS:
                    return
                for c in range(2):
                    part = slice(c * HALF, (c + 1) * HALF)
                    v.wait_ge(hi_ready, 2 * g + c + 1 + 8 * it)
                    nc.vector.tensor_tensor(w_lo[:, g % SLOTS, part], raw[:, g % RAW_SLOTS, part],
                                            w_hi[:, g % SLOTS, part].bitcast(F32), ALU.subtract).then_inc(lo_ready, 1)

            def y_low(b, d):
                t0 = SUBS[b].t_in
                v.wait_ge(yh_ready, KT * b + d + 1)
                nc.vector.scalar_tensor_tensor(
                    out=y_lo[:, d, t0:L], in0=xT[:, d, t0:L],
                    scalar=gains[:, SUBS[b].pre + d:SUBS[b].pre + d + 1],
                    in1=y_hi[:, d, t0:L].bitcast(F32), op0=ALU.mult, op1=ALU.subtract).then_inc(yl_ready, 1)

            def pre_norm(b):
                t = SUBS[b]
                t0 = t.t_in
                v.wait_ge(x_sq, 2 * b + 2)
                for n, m in enumerate((4, 2, 1)):
                    nc.vector.tensor_tensor(fT[:, 0:m, t0:L], fT[:, 0:m, t0:L], fT[:, m:2 * m, t0:L],
                                            ALU.add).then_inc(x_acc, 1)
                    v.wait_ge(x_acc, 3 * b + n + 1)
                conv_lo(t.g0 + 3)
                v.wait_ge(pre_sum, b + 1)
                nc.vector.tensor_scalar(pre_ms[:, t0:L], ps[:, BANK_PRE, t0:L], 1.0 / D, EPS,
                                        ALU.mult, ALU.add).then_inc(pre_var, 1)
                v.wait_ge(pre_var, b + 1)
                nc.vector.tensor_scalar(eps_ms[:, t0:L], pre_ms[:, t0:L], EPS, None, ALU.mult).then_inc(eps_ready, 1)
                v.wait_ge(eps_ready, b + 1)
                v.wait_ge(rms_ready, b + 1)

            conv_lo(0)
            for d in range(KT):
                v.wait_ge(x_turned, d + 1)
                nc.vector.tensor_copy(xT[:, d, :], ps[:, d, 0:L]).then_inc(x_ready, 1)
                if d == 0:
                    v.wait_ge(small_ready, 2)
                else:
                    y_low(0, d - 1)
            y_low(0, KT - 1)
            conv_lo(1)
            conv_lo(2)
            pre_norm(0)

            for t in SUBS:
                if t.kind == "ffn":
                    base = pairs_before[t.u]
                    t0 = t.t_in

                    def in_step(i, it):
                        j = i // 2
                        b0 = BANK_IN[i % 4][0]
                        v.wait_ge(panel_done, t.g0 + i + 1 + 4 * it)
                        if i % 2 == 0:
                            nc.vector.tensor_tensor(act[:, j % 2, :, t0:L], ps[:, b0:b0 + 2, t0:L],
                                                    spread(rms_inv, 2, t0), ALU.mult).then_inc(gate_ready, 1)
                            conv_lo(t.g0 + i + 4, it)
                        else:
                            v.wait_ge(silu_ready, base + j + 1 + 2 * it)
                            nc.vector.tensor_tensor(hid[:, j % 2, :, t0:L], act[:, j % 2, :, t0:L],
                                                    ps[:, b0:b0 + 2, t0:L], ALU.mult).then_inc(h_ready, 1)
                            conv_lo(t.g0 + i + 4, it)
                            v.wait_ge(hh_ready, base + j + 1 + 2 * it)
                            nc.vector.tensor_tensor(h_lo[:, bass.ds(2 * j + 4 * it, 2), t0:L],
                                                    hid[:, j % 2, :, t0:L],
                                                    h_hi[:, bass.ds(2 * j + 4 * it, 2), t0:L].bitcast(F32),
                                                    ALU.subtract).then_inc(hl_ready, 1)
                            v.wait_ge(hl_ready, base + j + 1 + 2 * it)
                    steps(v, 22, in_step)
                else:
                    def rope(b):
                        b0 = ROT_BANK[b]
                        v.wait_ge(rot_done, b + 1)
                        nc.vector.tensor_tensor(rot_s[:], ps[:, b0:b0 + 2, 0:L], spread(cst("sin"), 2, 0),
                                                ALU.mult).then_inc(rs_ready, 1)
                        v.wait_ge(rs_ready, b + 1)
                        v.wait_ge(rc_ready, b + 1)
                        nc.vector.tensor_tensor(qkv[:, 2 * b:2 * b + 2, :], rot_s[:], rot_c[:],
                                                ALU.add).then_inc(roped, 1)
                        v.wait_ge(roped, b + 1)

                    def drain(i, it):
                        b0 = BANK_IN[i % 4][0]
                        v.wait_ge(panel_done, t.g0 + i + 1 + 4 * it)
                        nc.vector.tensor_tensor(qkv[:, bass.ds(2 * i + 8 * it, 2), :], ps[:, b0:b0 + 2, 0:L],
                                                spread(rms_inv, 2, 0), ALU.mult).then_inc(proj_drained, 1)
                        if t.kind == "swa" and i == 3:
                            v.wait_ge(const_in_sem, 16)
                            rope(0)
                        if t.kind == "swa" and i == 4:
                            rope(1)
                            rope(2)
                        if (t.kind == "sb" and i < 11) or i < 2:
                            conv_lo(t.g0 + i + 4, it)
                        elif i == 3:
                            conv_lo(t.g0 + 6)
                            conv_lo(t.g0 + 7)
                    steps(v, 8 if t.kind == "sb" else 0, drain)
                    for i in range(8 if t.kind == "sb" else 0, t.n_in):
                        drain(i, 0)
                if t.kind == "sb":
                    v.wait_ge(const_in_sem, 16)
                    for st in range(NH + 6):
                        if st < NH:
                            v.wait_ge(z_done, st + 1)
                            if st >= 4:
                                v.wait_ge(d_ready, st - 3)
                            nc.vector.scalar_tensor_tensor(out=z[:, st % 4], in0=ps[:, st % 2, 0:SB_W],
                                                           scalar=SCALE, in1=cst("mask_sb"), op0=ALU.mult,
                                                           op1=ALU.add).then_inc(z_ready, 1)
                            v.wait_ge(z_ready, st + 1)
                            if st >= 2:
                                v.wait_ge(sp_ready, st - 1)
                            nc.vector.scalar_tensor_tensor(out=e[:, st % 2], in0=z[:, st % 4], scalar=-1.0,
                                                           in1=z[:, st % 4], op0=ALU.mult,
                                                           op1=ALU.min).then_inc(e_abs, 1)
                        if 1 <= st < NH + 1:
                            h = st - 1
                            v.wait_ge(e_ln, h + 1)
                            if h >= 2:
                                v.wait_ge(c_done, h - 1)
                            nc.vector.scalar_tensor_tensor(out=sp[:, h % 2, SB_PAD:], in0=z[:, h % 4], scalar=0.0,
                                                           in1=e[:, h % 2], op0=ALU.max,
                                                           op1=ALU.add).then_inc(sp_ready, 1)
                        if 1 <= st < 4:
                            n = 2 * st - 1
                            v.wait_ge(v_turned, n + 1)
                            nc.vector.tensor_copy(v_tok[:, n // 2, 512:1024], ps[:, 2 + n, :]).then_inc(v_saved_d, 1)
                        if 3 <= st < NH + 3:
                            h = st - 3
                            v.wait_ge(c_done, h + 1)
                            if h >= 3:
                                v.wait_ge(o_done, h - 2)
                            nc.vector.tensor_tensor(w[:, h % 3, SB_PAD:], z[:, h % 4], ps[:, 2 + h % 2, 0:SB_W],
                                                    ALU.subtract).then_inc(d_ready, 1)
                        if st >= 6 and (st - 6) % 2 == 0 and (st - 6) // 2 < 8:
                            q = (st - 6) // 2
                            v.wait_ge(oh_ready, q + 1)
                            nc.vector.tensor_tensor(y_lo[:, q, :], ps[:, 4 + q % 2, 0:L],
                                                    y_hi[:, q, :].bitcast(F32), ALU.subtract).then_inc(ol_ready, 1)
                    conv_lo(t.g_out + 3)
                elif t.kind == "swa":
                    v.wait_ge(const_in_sem, 16)

                    def mask_scores(h):
                        gq = h // GROUP
                        v.wait_ge(s_done, h + 1)
                        if gq >= 3:
                            v.wait_ge(pt_done, GROUP * (gq - 2))
                        nc.vector.scalar_tensor_tensor(out=s[:, gq % 3, h % GROUP], in0=ps[:, h % 4, 0:SW_W],
                                                       scalar=SCALE, in1=cst("mask_sw"), op0=ALU.mult,
                                                       op1=ALU.add).then_inc(s_ready, 1)

                    def maxima(gq, half):
                        q, hs = gq % 2, slice(2 * half, 2 * half + 2)
                        v.wait_ge(s_ready, GROUP * gq + 2 * half + 2)
                        for c in range(2):
                            nc.vector.tensor_reduce(top[:, q, c, hs],
                                                    s[:, gq % 3, hs, SW_COL[c]:SW_COL[c] + SW_KEYS[c]],
                                                    AX.X, ALU.max).then_inc(stat, 1)

                    def sink_maxima(gq):
                        q = gq % 2
                        v.wait_ge(stat, 5 * gq + 4)
                        sk = sinks[:, GROUP * gq:GROUP * gq + GROUP].unsqueeze(1).broadcast_to([P, 2, GROUP])
                        nc.vector.tensor_tensor(top[:, q], top[:, q], sk, ALU.max).then_inc(stat, 1)
                        v.wait_ge(stat, 5 * gq + 5)
                        nc.vector.tensor_scalar(neg[:, q], top[:, q], -1.0, None, ALU.mult).then_inc(top_ready, 1)
                        v.wait_ge(top_ready, gq + 1)
                        nc.vector.tensor_tensor(snk[:, q], neg[:, q], sk, ALU.add).then_inc(snk_sum, 1)

                    def normalise(gq, half):
                        q, hs = gq % 2, slice(2 * half, 2 * half + 2)
                        v.wait_ge(snk_exp, gq + 1)
                        v.wait_ge(p_exp, 8 * gq + 4 * half + 4)
                        nc.vector.tensor_tensor(den[:, q, :, hs], tot[:, q, :, hs], snk[:, q, :, hs], ALU.add)\
                            .then_inc(den_ready, 1)
                        v.wait_ge(den_ready, 2 * gq + half + 1)
                        nc.vector.reciprocal(inv[:, q, :, hs], den[:, q, :, hs]).then_inc(inv_ready, 1)
                        v.wait_ge(inv_ready, 2 * gq + half + 1)
                        for h in range(2 * half, 2 * half + 2):
                            for c in range(2):
                                k0, k1 = SW_COL[c], SW_COL[c] + SW_KEYS[c]
                                nc.vector.tensor_scalar(s[:, gq % 3, h, k0:k1], s[:, gq % 3, h, k0:k1],
                                                        inv[:, q, c, h:h + 1], None, ALU.mult).then_inc(p_ready, 1)

                    def save_o(q):
                        v.wait_ge(oh_ready, 8 + q + 1)
                        nc.vector.tensor_tensor(y_lo[:, q, META:L], ps[:, 6 + q % 2, 0:256],
                                                y_hi[:, q, META:L].bitcast(F32), ALU.subtract).then_inc(ol_ready, 1)

                    for st in range(NH + SW_LAG + 3):
                        if st < NH:
                            mask_scores(st)
                        if st % GROUP == 2 and st < NH:
                            maxima(st // GROUP, 0)
                        if st % GROUP == 0 and 1 <= st // GROUP <= NKV:
                            maxima(st // GROUP - 1, 1)
                            sink_maxima(st // GROUP - 1)
                        if st in ROPE_AT:
                            rope(ROPE_AT[st])
                        if st % GROUP == 3 and 1 <= st // GROUP <= NKV:
                            normalise(st // GROUP - 1, 0)
                        if st % GROUP == 1 and 2 <= st // GROUP <= NKV + 1:
                            normalise(st // GROUP - 2, 1)
                        h = st - SW_LAG
                        if h >= 3 and (h - 3) % 2 == 0 and (h - 3) // 2 < NH // 2:
                            save_o((h - 3) // 2)
                    conv_lo(t.g_out + 2)
                    conv_lo(t.g_out + 3)

                steps(v, n_split(t), lambda i, it: conv_lo(t.g_out + i + 4, it))
                k, t0 = t.u, t.t_out
                v.wait_ge(f_sq, 5 * k + 2)
                nc.vector.tensor_tensor(sq[:, 0:2, t0:L], sq[:, 0:2, t0:L], sq[:, 2:4, t0:L],
                                        ALU.add).then_inc(f_acc, 1)
                v.wait_ge(f_acc, 4 * k + 1)
                if t.kind == "ffn":
                    nc.vector.scalar_tensor_tensor(out=sq[:, 0, t0:L], in0=eps_ms[:, t0:L], scalar=float(KT),
                                                   in1=sq[:, 0, t0:L], op0=ALU.mult, op1=ALU.add).then_inc(f_acc, 1)
                else:
                    nc.vector.tensor_scalar(sq[:, 0, t0:L], sq[:, 0, t0:L], KT * EPS, None,
                                            ALU.add).then_inc(f_acc, 1)
                v.wait_ge(f_acc, 4 * k + 2)
                v.wait_ge(f_sq, 5 * k + 3)
                nc.vector.tensor_tensor(sq[:, 0:2, t0:L], sq[:, 0:2, t0:L], sq[:, 4:6, t0:L],
                                        ALU.add).then_inc(f_acc, 1)
                v.wait_ge(f_acc, 4 * k + 3)
                nc.vector.tensor_tensor(sq[:, 0, t0:L], sq[:, 0, t0:L], sq[:, 1, t0:L], ALU.add).then_inc(f_acc, 1)
                for d in range(6, 8):
                    v.wait_ge(f_sq, 5 * k + d - 2)
                    nc.vector.tensor_copy(fT[:, d, t0:L], ps[:, BANK_OUT[d], t0:L]).then_inc(f_saved2, 1)
                v.wait_ge(post_ready, k + 1)
                v.wait_ge(f_saved, 3 * k + 3)
                v.wait_ge(f_saved2, 2 * k + 2)

                def u_of(d):
                    if d < KT:
                        if d >= 2:
                            v.wait_ge(x_ready, KT * (k + 1) + d - 1)
                        nc.vector.tensor_tensor(scaled[:, d % 2, t0:L], fT[:, d, t0:L], post_f[:, t0:L],
                                                ALU.mult).then_inc(u_ready, 1)

                u_of(0)
                for d in range(KT):
                    if d > 0:
                        u_of(d + 1)
                    v.wait_ge(u_ready, KT * k + d + 1)
                    nc.vector.scalar_tensor_tensor(out=xT[:, d, t0:L], in0=scaled[:, d % 2, t0:L],
                                                   scalar=gains[:, t.post + d:t.post + d + 1],
                                                   in1=xT[:, d, t0:L], op0=ALU.mult,
                                                   op1=ALU.add).then_inc(x_ready, 1)
                    if d == 0:
                        if t.u < 5:
                            b = t.u + 1
                            v.wait_ge(x_ready, KT * b + 1)
                            nc.vector.tensor_scalar(y_hi[:, 0, SUBS[b].t_in:L], xT[:, 0, SUBS[b].t_in:L],
                                                    gains[:, SUBS[b].pre:SUBS[b].pre + 1], None,
                                                    ALU.mult).then_inc(yh_ready, 1)
                        u_of(1)
                    elif t.u < 5:
                        y_low(t.u + 1, d - 1)
                if t.u < 5:
                    y_low(t.u + 1, KT - 1)
                    pre_norm(t.u + 1)
                else:
                    c, half = OUT_PARTS[3]
                    v.wait_ge(out_turned, 4)
                    nc.vector.tensor_copy(x_rows(sq)[:, c, 512 * half:512 * half + 512], ps[:, 3, :]).then_inc(out_d, 1)

        @block.tensor
        def _(pe):
            def three(dst, slot, col, yh, yl, first, last):
                pc = slice(col, col + P)
                nc.tensor.matmul(dst, w_lo[:, slot, pc], yh, start=first, stop=False)
                nc.tensor.matmul(dst, w_hi[:, slot, pc], yh, start=False, stop=False)
                return nc.tensor.matmul(dst, w_hi[:, slot, pc], yl, start=False, stop=last)

            pe.wait_ge(few_landed, 16)
            pe.wait_ge(x_landed, 32)
            for d in range(KT):
                if d == 2:
                    pe.wait_ge(small_landed, 32)
                    nc.tensor.transpose(ps[:, 7, 288:288 + 96], g_rows[:], cst("ident", 96, 0, 96))
                    nc.tensor.matmul(ps[:, 7, 384:384 + NH], cst("ones", 1), s_row[:], start=True, stop=True)\
                        .then_inc(small_T, 1)
                if d == 7:
                    pe.wait_ge(small_ready, 2)
                nc.tensor.transpose(ps[:, d, 0:META], meta_rows(fT)[:, P * d:P * d + P], cst("ident", META, 0, META))
                for c in range(2):
                    mm = nc.tensor.transpose(ps[:, d, META + P * c:META + P * c + P],
                                             x_rows(sq)[:, c, P * d:P * d + P], cst("ident"))
                mm.then_inc(x_turned, 1)

            for t in SUBS:
                t0 = t.t_in
                head = HEAD if t.u else 1
                for k in range(KT):
                    if k == KT - 1 and t.u:
                        pe.wait_ge(x_acc, 3 * t.u + 3)
                        nc.tensor.matmul(ps[:, BANK_PRE, t0:L], cst("ones"), fT[:, 0, t0:L],
                                         start=True, stop=True).then_inc(pre_sum, 1)
                    pe.wait_ge(yh_ready, KT * t.u + k + 1)
                    if t.u == 0 and k == 0:
                        pe.wait_ge(x_ready, 2)
                    if k < KT - 1:
                        for i in range(head):
                            g = t.g0 + i
                            if k in (0, 4):
                                pe.wait_ge(lo_ready, 2 * g + 1 + k // 4)
                            for c in range(2):
                                dst = ps[:, BANK_IN[i][c], t0:L]
                                pc = slice(256 * k + P * c, 256 * k + P * c + P)
                                nc.tensor.matmul(dst, w_lo[:, g % SLOTS, pc], y_hi[:, k, t0:L],
                                                 start=(k == 0), stop=False)
                                nc.tensor.matmul(dst, w_hi[:, g % SLOTS, pc], y_hi[:, k, t0:L],
                                                 start=False, stop=False)
                        pe.wait_ge(yl_ready, KT * t.u + k + 1)
                        for i in range(head):
                            g = t.g0 + i
                            for c in range(2):
                                pc = slice(256 * k + P * c, 256 * k + P * c + P)
                                nc.tensor.matmul(ps[:, BANK_IN[i][c], t0:L], w_hi[:, g % SLOTS, pc],
                                                 y_lo[:, k, t0:L], start=False, stop=False)
                    else:
                        pe.wait_ge(yl_ready, KT * t.u + k + 1)
                        for i in range(head):
                            g = t.g0 + i
                            for c in range(2):
                                mm = three(ps[:, BANK_IN[i][c], t0:L], g % SLOTS, 256 * k + P * c,
                                           y_hi[:, k, t0:L], y_lo[:, k, t0:L], False, True)
                            mm.then_inc(panel_done, 1)

                def in_panel(i, it):
                    g = t.g0 + i
                    pe.wait_ge(lo_ready, 2 * g + 2 + 8 * it)
                    if i < 3:
                        pass
                    elif i == 3:
                        pe.wait_ge(pre_var, t.u + 1)
                    elif t.kind == "ffn":
                        done, n = (gate_ready, h_ready)[i % 2], pairs_before[t.u] + (i - 4) // 2 + 1
                        pe.wait_ge(done, n + 2 * it)
                    else:
                        pe.wait_ge(proj_drained, drained_before[t.u] + i - 3 + 4 * it)
                    for c in range(2):
                        for k in range(KT):
                            mm = three(ps[:, BANK_IN[i % 4][c], t0:L], g % SLOTS, 256 * k + P * c,
                                       y_hi[:, k, t0:L], y_lo[:, k, t0:L], k == 0, k == KT - 1)
                    mm.then_inc(panel_done, 1)

                def rotate(b):
                    if b == 0:
                        pe.wait_ge(const_in_sem, 16)
                    pe.wait_ge(proj_drained, drained_before[4] + (3, 4, 4, 4, 5)[b])
                    if b >= 2:
                        pe.wait_ge(rs_ready, b - 1)
                    for c in range(2):
                        mm = nc.tensor.matmul(ps[:, ROT_BANK[b] + c, 0:L], cst("rot"), qkv[:, 2 * b + c, :],
                                              start=True, stop=True)
                    mm.then_inc(rot_done, 1)

                for i in range(head, 3):
                    in_panel(i, 0)
                if t.u == 0:
                    pe.wait_ge(x_acc, 3)
                    nc.tensor.matmul(ps[:, BANK_PRE, t0:L], cst("ones"), fT[:, 0, t0:L],
                                     start=True, stop=True).then_inc(pre_sum, 1)
                in_panel(3, 0)
                if t.kind == "swa":
                    rotate(0)
                    in_panel(4, 0)
                    rotate(1)
                    rotate(2)
                    in_panel(5, 0)
                else:
                    steps(pe, t.n_in - 4, lambda i, it: in_panel(i + 4, it))

                if t.kind == "sb":
                    qd = drained_before[t.u]

                    def scores(h):
                        r = slice(HD * (h % 2), HD * (h % 2) + HD)
                        if h >= 2:
                            pe.wait_ge(z_ready, h - 1)
                        for n in (2, 0, 1):
                            k0, width = SB_KEY[n], max(L - SB_Q0[n], P)
                            queries = qkv[r, h // 2:h // 2 + 2, :].rearrange("p a t -> p (a t)")
                            mm = nc.tensor.matmul(ps[:, h % 2, SB_COL[n]:SB_COL[n] + width],
                                                  qkv[r, KT + h // 2, k0:k0 + P],
                                                  queries[:, SB_Q0[n]:SB_Q0[n] + width], start=True, stop=True)
                        mm.then_inc(z_done, 1)

                    def running_sums(h):
                        pe.wait_ge(sp_ready, h + 1)
                        if h >= 2:
                            pe.wait_ge(d_ready, h - 1)
                        else:
                            pe.wait_ge(v_saved_a, 1)
                            pe.wait_ge(v_saved_d, 1)
                        for n, m in ((2, 2), (0, 0), (0, 1), (0, 2), (1, 1), (1, 2)):
                            at, src = SB_COL[n] + SB_Q0[m] - SB_Q0[n], SB_PAD + SB_COL[m]
                            back = SB_PAD if m == 2 and n < 2 else 0
                            width = max(L - SB_Q0[m], P) - back
                            mm = nc.tensor.matmul(ps[:, 2 + h % 2, at - back:at + width],
                                                  cst("tri" if m == n else "ones"),
                                                  sp[:, h % 2, src - back:src + width],
                                                  start=(m == n), stop=(m == 2), skip_group_check=True)
                        mm.then_inc(c_done, 1)

                    def values(h):
                        pe.wait_ge(w_ready, h + 1)
                        q = h // 2
                        if h == 0:
                            pe.wait_ge(v_saved_a, 3)
                            pe.wait_ge(v_saved_d, 3)
                        if q >= 2:
                            pe.wait_ge(ol_ready, q - 1)
                        r = slice(HD * (h % 2), HD * (h % 2) + HD)
                        for n in range(3):
                            back = SB_PAD if n == 2 else 0
                            src = SB_PAD + SB_COL[n]
                            mm = nc.tensor.matmul(ps[r, 4 + q % 2, SB_Q0[n] - back:L],
                                                  v_tok[:, n, HD * h:HD * h + HD],
                                                  w[:, h % 3, src - back:src + L - SB_Q0[n]],
                                                  start=(n == 0), stop=(n == 2), skip_group_check=True)
                        mm.then_inc(o_done, 1)

                    pe.wait_ge(const_in_sem, 16)
                    pe.wait_ge(pad_zero, 2)
                    pe.wait_ge(proj_drained, qd + 12)
                    scores(0)
                    scores(1)
                    for n in range(6):
                        for c in range(4):
                            mm = nc.tensor.transpose(
                                ps[:, 2 + n, P * c:P * c + P],
                                qkv[:, 2 * KT + 4 * (n % 2) + c, SB_KEY[n // 2]:SB_KEY[n // 2] + P], cst("ident"))
                        mm.then_inc(v_turned, 1)
                    for st in range(2, NH + 4):
                        if st < NH:
                            scores(st)
                        if 2 <= st < NH + 2:
                            running_sums(st - 2)
                        if 4 <= st:
                            values(st - 4)
                elif t.kind == "swa":
                    def scores(h):
                        r = slice(HD * (h % 2), HD * (h % 2) + HD)
                        kv = h // GROUP
                        if h % 4 == 0:
                            pe.wait_ge(roped, 2 + h // 4)
                            pe.wait_ge(kd_ready, 12)
                        if h >= 4:
                            pe.wait_ge(s_ready, h - 3)
                        for c in range(2):
                            mm = nc.tensor.matmul(ps[:, h % 4, SW_COL[c]:SW_COL[c] + SW_KEYS[c]],
                                                  qkv[r, 2 + h // 2, META + P * c:META + P * c + P],
                                                  kd[r, kv, SW_COL[c]:SW_COL[c] + SW_KEYS[c]], start=True, stop=True)
                        mm.then_inc(s_done, 1)

                    def turn(h):
                        pr = s[:, h // GROUP % 3, h % GROUP]
                        pe.wait_ge(p_ready, 2 * h + 2)
                        if h >= 2:
                            pe.wait_ge(pt_saved, h - 1)
                        elif h == 0:
                            pe.wait_ge(rs_ready, 5)
                        for n, (c, k0, _) in enumerate(SW_WIN):
                            mm = nc.tensor.transpose(ps[:, 4 + h % 2, P * n:P * n + P],
                                                     pr[:, SW_COL[c] + k0:SW_COL[c] + k0 + P], cst("ident"))
                        mm.then_inc(pt_done, 1)

                    def values(h):
                        q = h // 2
                        r = slice(HD * (h % 2), HD * (h % 2) + HD)
                        vc = slice(HD * (h // GROUP), HD * (h // GROUP) + HD)
                        pe.wait_ge(pt_saved, h + 1)
                        if h == 0:
                            pe.wait_ge(v_saved_a, 5)
                        if q >= 2:
                            pe.wait_ge(ol_ready, 8 + q - 1)
                        for n, (c, _, zero) in enumerate(SW_WIN):
                            mm = nc.tensor.matmul(ps[r, 6 + q % 2, P * c:P * c + P], vt[:, n, vc],
                                                  p_t[:, h % 2, P * n:P * n + P], start=(zero == 0),
                                                  stop=(zero > 0))
                        mm.then_inc(o_done, 1)

                    def turn_v():
                        pe.wait_ge(win_ready, 4)
                        pe.wait_ge(rs_ready, 4)
                        for n in range(4):
                            for c in range(2):
                                at = 256 * (n % 2) + P * c
                                mm = nc.tensor.transpose(ps[:, 6 + n // 2, at:at + P], v_win[:, c, n, :], cst("ident"))
                            if n % 2:
                                mm.then_inc(v_turned, 1)

                    rotate(3)
                    rotate(4)
                    pe.wait_ge(proj_drained, drained_before[4] + 6)
                    for st in range(NH + SW_LAG + 1):
                        if st < NH:
                            scores(st)
                        if st == 6:
                            turn_v()
                        if 0 <= st - SW_LAG < NH:
                            turn(st - SW_LAG)
                        if st - SW_LAG >= 1:
                            values(st - SW_LAG - 1)

                t0 = t.t_out
                src_hi, src_lo = (h_hi, h_lo) if t.kind == "ffn" else (y_hi, y_lo)

                def out_panel(i, it, first=False, last=False):
                    g = t.g_out + i
                    pe.wait_ge(lo_ready, 2 * g + 2 + 8 * it)
                    if t.kind == "ffn":
                        pe.wait_ge(hl_ready, pairs_before[t.u] + i + 1 + 4 * it)
                    elif first:
                        pe.wait_ge(ol_ready, 8 if t.kind == "sb" else 16)
                    for d in range(KT):
                        if first and t.kind == "ffn" and d % 2 == 0:
                            pe.wait_ge((gate_ready, h_ready)[d // 2 % 2], pairs_before[t.u] + 10 + d // 4)
                        for c in range(2):
                            mm = three(ps[:, BANK_OUT[d], t0:L], g % SLOTS, D * c + P * d,
                                       src_hi[:, 2 * i + c + 8 * it, t0:L], src_lo[:, 2 * i + c + 8 * it, t0:L],
                                       first and c == 0, last and c == 1)
                        if last:
                            mm.then_inc(f_done, 1)
                    if last:
                        post_sums()
                    else:
                        mm.then_inc(panel_done, 1)

                def post_sums():
                    pe.wait_ge(f_saved, 3 * t.u + 2)
                    for d in (6, 7, 0):
                        if d == 0:
                            pe.wait_ge(f_acc, 4 * t.u + 4)
                        else:
                            pe.wait_ge(f_sq, 5 * t.u + d - 2)
                        mm = nc.tensor.matmul(ps[:, BANK_POST, t0:L], cst("ones"), sq[:, d, t0:L],
                                              start=(d == 6), stop=(d == 0))
                        if d == 6:
                            mm.then_inc(panel_done, 1)
                    mm.then_inc(post_sum, 1)

                out_panel(0, 0, first=True)
                steps(pe, t.n_out - 2, lambda i, it: out_panel(i + 1, it))
                out_panel(t.n_out - 1, 0, last=True)
            for d in range(KT):
                pe.wait_ge(x_ready, KT * 6 + d + 1)
                for n, (a, half) in enumerate(OUT_PARTS):
                    if half == d // 4:
                        mm = nc.tensor.transpose(ps[:, n, P * (d % 4):P * (d % 4) + P],
                                                 xT[:, d, META + P * a:META + P * a + P], cst("ident"))
                        if d % 4 == 3:
                            mm.then_inc(out_turned, 1)


_INS = ["x", "meta_tokens", "norm_g", "ffn_w_gate", "ffn_w_up", "ffn_w_down", "sb_w_in", "sb_w_out",
        "swa_w_in", "swa_sinks", "swa_w_out"]


def constants():
    c = np.zeros((P, CONST_W), np.float32)

    def part(name):
        lo, hi = CONST[name]
        return c[:, lo:hi]

    p = np.arange(P)
    for n in range(3):
        q = np.arange(SB_Q0[n], L)
        key = SB_KEY[n] + p
        seen = (key[:, None] < q[None, :]) & (key[:, None] >= (256 if n == 2 else 0))
        part("mask_sb")[:, SB_COL[n]:SB_COL[n] + len(q)] = np.where(seen, 0, HIDDEN)
    part("tri")[:] = p[:, None] >= p[None, :]
    part("ident")[:] = np.eye(P)
    part("ones")[:] = 1
    for n in range(2):
        key = np.array(SW_TOKENS[n])
        key_chunk = np.where(key < META, -1, (key - META) // CHUNK)
        own = (2 * n + p // CHUNK)[:, None]
        seen = (key_chunk == -1) | ((key_chunk >= own - 1) & (key_chunk <= own))
        part("mask_sw")[:, SW_COL[n]:SW_COL[n] + len(key)] = np.where(seen, 0, HIDDEN)
    first = p % HD < HD // 2
    part("rot")[np.where(first, p + HD // 2, p - HD // 2), p] = np.where(first, -1, 1)
    freq = np.float32(THETA) ** (-np.arange(HD // 2, dtype=np.float32) / np.float32(HD // 2))
    angle = np.arange(L, dtype=np.float32)[None, :] * freq[p % (HD // 2)][:, None]
    part("cos")[:] = np.cos(angle)
    part("sin")[:] = np.sin(angle)
    return c


def kernel(**inputs):
    import numpy as _np
    import concourse.bacc as _bacc
    from concourse import mybir as _mybir
    from concourse.bass_utils import run_bass_kernel_spmd as _run

    nc = _bacc.Bacc("TRN2", target_bir_lowering=False, num_devices=1)
    arrays, args = {}, []
    for name in _INS:
        a = _np.ascontiguousarray(inputs[name])
        arrays[f"in_{name}_dram"] = a
        args.append(nc.dram_tensor(f"in_{name}_dram", a.shape, _mybir.dt.from_np(a.dtype), kind="ExternalInput").ap())
    c = constants()
    arrays["const_dram"] = c
    args.append(nc.dram_tensor("const_dram", c.shape, F32, kind="ExternalInput").ap())
    args.append(nc.dram_tensor("out_0_dram", (1, SEQ, D), F32, kind="ExternalOutput").ap())
    x, *rest, out = args
    build(nc, x.rearrange("b s d -> (b s) d"), *rest, out.rearrange("b s d -> (b s) d"))
    r = _run(nc, [arrays], core_ids=[0])
    return r.results[0]["out_0_dram"]
```
